# Optimizing a Trainium2 kernel written in Bass

```python
import math
import jax, jax.numpy as jnp
from jax import lax
import numpy as np

D_MODEL = 1024
BATCH = 1
SEQ = 256
DEPTH = 1

D_MIX = D_MODEL
N_MIXERS = 4
GROUP_W = D_MIX // N_MIXERS
CONF_KERNEL = 31
CONF_GROUPS = 4
GN_EPS = 1e-5
SCONV_KERNEL = 3
ATT_HEADS = 4
HEAD_DIM = GROUP_W // ATT_HEADS
MOBA_BLOCK = 256
MOBA_TOP_K = 3
Q_BLOCK = 128
LRU_BLOCKS = 4
LRU_BLOCK_W = GROUP_W // LRU_BLOCKS
LRU_CONV = 4
LRU_C = 8.0
D_FF = 4 * D_MODEL
RMS_EPS = 1e-6
CONF_COLS = 2 * GROUP_W
SC_COLS = 3 * GROUP_W
ATT_COLS = 3 * GROUP_W
LRU_COLS = 2 * GROUP_W
IN_COLS = CONF_COLS + SC_COLS + ATT_COLS + LRU_COLS


def rms_norm(x, g):
    xf = x.astype(jnp.float32)
    y = xf * lax.rsqrt(jnp.mean(xf * xf, axis=-1, keepdims=True) + RMS_EPS)
    return (y * g.astype(jnp.float32)).astype(x.dtype)

def causal_depthwise_conv(x, w):
    k_w, c = w.shape
    return lax.conv_general_dilated(
        x, w[:, None, :].astype(x.dtype), window_strides=(1,), padding=[(k_w - 1, 0)],
        dimension_numbers=("NWC", "WIO", "NWC"), feature_group_count=c)

def group_norm_channels(x, g, b):
    bsz, s, c = x.shape
    xf = x.astype(jnp.float32).reshape(bsz, s, CONF_GROUPS, c // CONF_GROUPS)
    mu = jnp.mean(xf, axis=-1, keepdims=True)
    var = jnp.mean(jnp.square(xf - mu), axis=-1, keepdims=True)
    y = ((xf - mu) * lax.rsqrt(var + GN_EPS)).reshape(bsz, s, c)
    return (y * g.astype(jnp.float32) + b.astype(jnp.float32)).astype(x.dtype)

def conformer_conv_mixer(u, dw_w, dw_b, gn_g, gn_b):
    val, gate = jnp.split(u, 2, axis=-1)
    z = val * jax.nn.sigmoid(gate)
    z = causal_depthwise_conv(z, dw_w) + dw_b
    z = group_norm_channels(z, gn_g, gn_b)
    return jax.nn.silu(z)

def short_conv_mixer(u, conv_w):
    b_gate, c_gate, xs = jnp.split(u, 3, axis=-1)
    return b_gate * causal_depthwise_conv(c_gate * xs, conv_w)

def block_diag(x, w, b):
    bsz, s, c = x.shape
    xg = x.reshape(bsz, s, LRU_BLOCKS, LRU_BLOCK_W)
    return jnp.einsum("bsgi,gij->bsgj", xg, w).reshape(bsz, s, c) + b

def rglru_mixer(u, conv_w, conv_b, wa, ba, wx, bx, lam):
    xr, gate = jnp.split(u, 2, axis=-1)
    xc = causal_depthwise_conv(xr, conv_w) + conv_b
    r = jax.nn.sigmoid(block_diag(xc, wa, ba).astype(jnp.float32))
    i = jax.nn.sigmoid(block_diag(xc, wx, bx).astype(jnp.float32))
    log_a = -LRU_C * r * jax.nn.softplus(-lam.astype(jnp.float32))
    a = jnp.exp(log_a)
    mult = jnp.sqrt(-jnp.expm1(2.0 * log_a))
    bterm = mult * (i * xc.astype(jnp.float32))

    def combine(e1, e2):
        a1, b1 = e1
        a2, b2 = e2
        return a1 * a2, a2 * b1 + b2

    _, h = lax.associative_scan(combine, (a, bterm), axis=1)
    return (h * jax.nn.gelu(gate.astype(jnp.float32))).astype(u.dtype)

def moba_attention(u):
    bsz, s, _ = u.shape
    q, k, v = jnp.split(u.astype(jnp.float32), 3, axis=-1)
    q = q.reshape(bsz, s, ATT_HEADS, HEAD_DIM).transpose(0, 2, 1, 3) * (HEAD_DIM ** -0.5)
    k = k.reshape(bsz, s, ATT_HEADS, HEAD_DIM)
    v = v.reshape(bsz, s, ATT_HEADS, HEAD_DIM)
    nb = -(-s // MOBA_BLOCK)
    pad = nb * MOBA_BLOCK - s
    kp = jnp.pad(k, ((0, 0), (0, pad), (0, 0), (0, 0)))
    vp = jnp.pad(v, ((0, 0), (0, pad), (0, 0), (0, 0)))
    kb = kp.reshape(bsz, nb, MOBA_BLOCK, ATT_HEADS, HEAD_DIM).transpose(0, 3, 1, 2, 4)
    vb = vp.reshape(bsz, nb, MOBA_BLOCK, ATT_HEADS, HEAD_DIM).transpose(0, 3, 1, 2, 4)
    slopes = 2.0 ** (-8.0 * jnp.arange(1, ATT_HEADS + 1, dtype=jnp.float32) / ATT_HEADS)

    kmean = jnp.mean(kb, axis=3)
    gate = jnp.einsum("bhsd,bhnd->bhsn", q, kmean)
    q_blk = jnp.arange(s) // MOBA_BLOCK
    past = jnp.arange(nb)[None, :] < q_blk[:, None]
    gate = jnp.where(past, gate, -jnp.inf)
    topk = max(min(MOBA_TOP_K, nb - 1), 1)
    _, idx = lax.top_k(gate, topk)

    nq = s // Q_BLOCK
    q_c = q.reshape(bsz, ATT_HEADS, nq, Q_BLOCK, HEAD_DIM).transpose(0, 2, 1, 3, 4)
    q_c = q_c.reshape(bsz * nq, ATT_HEADS, Q_BLOCK, HEAD_DIM)
    i_c = idx.reshape(bsz, ATT_HEADS, nq, Q_BLOCK, topk).transpose(0, 2, 1, 3, 4)
    i_c = i_c.reshape(bsz * nq, ATT_HEADS, Q_BLOCK, topk)
    b_ids = jnp.repeat(jnp.arange(bsz), nq)
    n_ids = jnp.tile(jnp.arange(nq), bsz)
    hh = jnp.arange(ATT_HEADS)[:, None, None]
    offs = jnp.arange(MOBA_BLOCK)

    def one_block(args):
        qc, ic, b, n = args
        kbb = kb[b]
        vbb = vb[b]
        t = n * Q_BLOCK + jnp.arange(Q_BLOCK)
        own = (n * Q_BLOCK) // MOBA_BLOCK
        k_own = kbb[:, own]
        v_own = vbb[:, own]
        s_pos = own * MOBA_BLOCK + offs
        d_own = (t[:, None] - s_pos[None, :]).astype(jnp.float32)
        s_own = jnp.einsum("hqd,hkd->hqk", qc, k_own) - slopes[:, None, None] * d_own
        s_own = jnp.where(d_own >= 0, s_own, -jnp.inf)
        kg = kbb[hh, ic]
        vg = vbb[hh, ic]
        sel_pos = ic[..., None] * MOBA_BLOCK + offs
        d_sel = (t[None, :, None, None] - sel_pos).astype(jnp.float32)
        s_sel = jnp.einsum("hqd,hqjkd->hqjk", qc, kg) - slopes[:, None, None, None] * d_sel
        s_sel = jnp.where((ic < own)[..., None], s_sel, -jnp.inf)
        scores = jnp.concatenate([s_sel.reshape(ATT_HEADS, Q_BLOCK, topk * MOBA_BLOCK), s_own], axis=-1)
        p = jax.nn.softmax(scores, axis=-1)
        p_sel = p[..., : topk * MOBA_BLOCK].reshape(ATT_HEADS, Q_BLOCK, topk, MOBA_BLOCK)
        p_own = p[..., topk * MOBA_BLOCK:]
        return (jnp.einsum("hqjk,hqjkd->hqd", p_sel, vg)
                + jnp.einsum("hqk,hkd->hqd", p_own, v_own))

    out = lax.map(one_block, (q_c, i_c, b_ids, n_ids))
    out = out.reshape(bsz, nq, ATT_HEADS, Q_BLOCK, HEAD_DIM).transpose(0, 1, 3, 2, 4)
    return out.reshape(bsz, s, GROUP_W).astype(u.dtype)

def first_inputs(seed: int = 0) -> dict:
    key = jax.random.key(seed)
    ks = jax.random.split(key, 24)
    f32 = jnp.float32

    def nrm(k, shape, scale):
        return jax.random.normal(k, shape, f32) * scale

    def gain(k, shape):
        return 1.0 + 0.05 * jax.random.normal(k, shape, f32)

    u = jax.random.uniform(ks[20], (DEPTH, GROUP_W), f32, 0.9, 0.999)
    base = u ** (1.0 / LRU_C)
    lru_lam = jnp.log(base) - jnp.log1p(-base)
    return {
        "x": jax.random.normal(ks[0], (BATCH, SEQ, D_MODEL), f32),
        "pre_mix_g": gain(ks[1], (DEPTH, D_MODEL)),
        "w_in": nrm(ks[2], (DEPTH, D_MODEL, IN_COLS), D_MODEL ** -0.5),
        "conf_dw_w": nrm(ks[3], (DEPTH, CONF_KERNEL, GROUP_W), CONF_KERNEL ** -0.5),
        "conf_dw_b": nrm(ks[4], (DEPTH, GROUP_W), 0.02),
        "conf_gn_g": gain(ks[5], (DEPTH, GROUP_W)),
        "conf_gn_b": nrm(ks[6], (DEPTH, GROUP_W), 0.02),
        "sconv_w": nrm(ks[7], (DEPTH, SCONV_KERNEL, GROUP_W), SCONV_KERNEL ** -0.5),
        "lru_conv_w": nrm(ks[8], (DEPTH, LRU_CONV, GROUP_W), LRU_CONV ** -0.5),
        "lru_conv_b": nrm(ks[9], (DEPTH, GROUP_W), 0.02),
        "lru_wa": nrm(ks[10], (DEPTH, LRU_BLOCKS, LRU_BLOCK_W, LRU_BLOCK_W), LRU_BLOCK_W ** -0.5),
        "lru_ba": nrm(ks[11], (DEPTH, GROUP_W), 0.02),
        "lru_wx": nrm(ks[12], (DEPTH, LRU_BLOCKS, LRU_BLOCK_W, LRU_BLOCK_W), LRU_BLOCK_W ** -0.5),
        "lru_bx": nrm(ks[13], (DEPTH, GROUP_W), 0.02),
        "lru_lam": lru_lam,
        "w_out": nrm(ks[14], (DEPTH, D_MIX, D_MODEL), D_MIX ** -0.5),
        "post_mix_g": gain(ks[15], (DEPTH, D_MODEL)),
        "pre_mlp_g": gain(ks[16], (DEPTH, D_MODEL)),
        "mlp_w1": nrm(ks[17], (DEPTH, D_MODEL, D_FF), D_MODEL ** -0.5),
        "mlp_w2": nrm(ks[18], (DEPTH, D_FF, D_MODEL), D_FF ** -0.5),
        "post_mlp_g": gain(ks[19], (DEPTH, D_MODEL)),
    }

def first_block(x, pre_mix_g, w_in, conf_dw_w, conf_dw_b, conf_gn_g, conf_gn_b, sconv_w,
              lru_conv_w, lru_conv_b, lru_wa, lru_ba, lru_wx, lru_bx, lru_lam, w_out,
              post_mix_g, pre_mlp_g, mlp_w1, mlp_w2, post_mlp_g):
    splits = [CONF_COLS, CONF_COLS + SC_COLS, CONF_COLS + SC_COLS + ATT_COLS]
    for l in range(DEPTH):
        h = rms_norm(x, pre_mix_g[l])
        u = h @ w_in[l]
        u_conf, u_sc, u_att, u_lru = jnp.split(u, splits, axis=-1)
        y_a = conformer_conv_mixer(u_conf, conf_dw_w[l], conf_dw_b[l], conf_gn_g[l], conf_gn_b[l])
        y_b = short_conv_mixer(u_sc, sconv_w[l])
        y_c = moba_attention(u_att)
        y_d = rglru_mixer(u_lru, lru_conv_w[l], lru_conv_b[l], lru_wa[l], lru_ba[l],
                          lru_wx[l], lru_bx[l], lru_lam[l])
        y = jnp.concatenate([y_a, y_b, y_c, y_d], axis=-1) @ w_out[l]
        x = x + rms_norm(y, post_mix_g[l])
        h = rms_norm(x, pre_mlp_g[l])
        m = jnp.square(jax.nn.relu(h @ mlp_w1[l])) @ mlp_w2[l]
        x = x + rms_norm(m, post_mlp_g[l])
    return x


DEPTH_2 = 2

N_META = 16
N_A_LAYERS = DEPTH_2 // 2
N_B_LAYERS = DEPTH_2 - N_A_LAYERS
POOL_WINDOWS = (2, 4, 8, 16)
POOL_GROUP = D_MODEL // len(POOL_WINDOWS)
SB_HEADS = 16
SB_HEAD_DIM = D_MODEL // SB_HEADS
PEER_HEADS = 8
PEER_N_KEYS = 128
PEER_N_EXPERTS = PEER_N_KEYS * PEER_N_KEYS
PEER_TOPK = 16
PEER_QUERY_DIM = 256
PEER_HALF = PEER_QUERY_DIM // 2
PEER_CHUNK = 16
EPS = 1e-6


def rmsnorm(x, g):
    xf = x.astype(jnp.float32)
    y = xf * lax.rsqrt(jnp.mean(xf * xf, axis=-1, keepdims=True) + EPS)
    return (y * g.astype(jnp.float32)).astype(x.dtype)

def pool_mixer(h, w_pool, scale):
    L = h.shape[1]
    hf = h.astype(jnp.float32)
    pos = jnp.arange(L)
    outs = []
    for g, w in enumerate(POOL_WINDOWS):
        hg = hf[..., g * POOL_GROUP:(g + 1) * POOL_GROUP]
        c = jnp.cumsum(hg, axis=1)
        c_prev = jnp.pad(c, ((0, 0), (w, 0), (0, 0)))[:, :L]
        cnt = jnp.minimum(pos + 1, w).astype(jnp.float32)[None, :, None]
        pooled = ((c - c_prev) / cnt - hg).astype(h.dtype)
        outs.append(jnp.einsum('bsc,cd->bsd', pooled, w_pool[g]))
    return jnp.concatenate(outs, axis=-1) * scale

def stick_breaking(q, k, v):
    B, L, H, dh = q.shape
    pad = (-L) % Q_BLOCK
    Lp = L + pad
    nblk = Lp // Q_BLOCK
    pw = ((0, 0), (pad, 0), (0, 0), (0, 0))
    qb = jnp.pad(q, pw).reshape(B, nblk, Q_BLOCK, H, dh).transpose(1, 0, 3, 2, 4)
    kp = jnp.pad(k, pw).transpose(0, 2, 1, 3)
    vp = jnp.pad(v, pw).transpose(0, 2, 1, 3)
    key_pos = jnp.arange(Lp)
    key_real = key_pos >= pad
    scale = SB_HEAD_DIM ** -0.5

    def block(args):
        q_blk, i = args
        q_pos = i * Q_BLOCK + jnp.arange(Q_BLOCK)
        z = jnp.einsum('bhqd,bhkd->bhqk', q_blk, kp,
                       preferred_element_type=jnp.float32) * scale
        valid = (key_pos[None, :] < q_pos[:, None]) & key_real[None, :]
        log_keep = jnp.where(valid, jax.nn.log_sigmoid(-z), 0.0)
        after = lax.cumsum(log_keep, axis=3, reverse=True) - log_keep
        log_w = jax.nn.log_sigmoid(z) + after
        wgt = jnp.where(valid, jnp.exp(log_w), 0.0)
        return jnp.einsum('bhqk,bhkd->bqhd', wgt.astype(v.dtype), vp)

    out = lax.map(block, (qb, jnp.arange(nblk)))
    out = out.transpose(1, 0, 2, 3, 4).reshape(B, Lp, H * dh)
    return out[:, pad:]

def peer(h, w_query, sub_keys, u, v):
    B, L, D = h.shape
    nchunk = L // PEER_CHUNK
    hc = h.reshape(B, nchunk, PEER_CHUNK, D).transpose(1, 0, 2, 3)

    def chunk(hx):
        q = jnp.einsum('btd,dq->btq', hx, w_query).reshape(
            B, PEER_CHUNK, PEER_HEADS, 2, PEER_HALF)
        s = jnp.einsum('bthpc,hpnc->bthpn', q, sub_keys,
                       preferred_element_type=jnp.float32)
        top_s, top_i = lax.top_k(s, PEER_TOPK)
        cand_s = (top_s[..., 0, :, None] + top_s[..., 1, None, :]).reshape(
            B, PEER_CHUNK, PEER_HEADS, PEER_TOPK * PEER_TOPK)
        cand_i = (top_i[..., 0, :, None] * PEER_N_KEYS + top_i[..., 1, None, :]).reshape(
            B, PEER_CHUNK, PEER_HEADS, PEER_TOPK * PEER_TOPK)
        best_s, best_pos = lax.top_k(cand_s, PEER_TOPK)
        expert = jnp.take_along_axis(cand_i, best_pos, axis=-1)
        gate = jax.nn.softmax(best_s, axis=-1)
        u_sel = jnp.take(u, expert, axis=0)
        v_sel = jnp.take(v, expert, axis=0)
        act = jax.nn.gelu(jnp.einsum('btd,bthkd->bthk', hx, u_sel,
                                     preferred_element_type=jnp.float32), approximate=False)
        return jnp.einsum('bthk,bthkd->btd', (gate * act).astype(h.dtype), v_sel)

    y = lax.map(chunk, hc)
    return y.transpose(1, 0, 2, 3).reshape(B, L, D)

def second_inputs(seed: int = 0) -> dict:
    key = jax.random.key(seed)
    ks = jax.random.split(key, 16)
    f = jnp.float32
    D = D_MODEL
    nrm = lambda k, shape, s: jax.random.normal(k, shape, f) * s
    return {
        "x": jax.random.normal(ks[0], (BATCH, SEQ, D), f),
        "meta_tokens": nrm(ks[1], (N_META, D), 1.0),
        "norm_mix": 1.0 + nrm(ks[2], (DEPTH_2, D), 0.02),
        "norm_ffn": 1.0 + nrm(ks[3], (DEPTH_2, D), 0.02),
        "pool_w": nrm(ks[4], (N_A_LAYERS, len(POOL_WINDOWS), POOL_GROUP, POOL_GROUP), POOL_GROUP ** -0.5),
        "pool_scale": 0.5 + nrm(ks[5], (N_A_LAYERS, D), 0.05),
        "kv_norm": 1.0 + nrm(ks[6], (D,), 0.02),
        "w_kv": nrm(ks[7], (D, 2 * D), D ** -0.5),
        "k_norm": 1.0 + nrm(ks[8], (SB_HEAD_DIM,), 0.02),
        "w_q": nrm(ks[9], (N_B_LAYERS, D, D), D ** -0.5),
        "q_norm": 1.0 + nrm(ks[10], (N_B_LAYERS, SB_HEAD_DIM), 0.02),
        "w_o": nrm(ks[11], (N_B_LAYERS, D, D), D ** -0.5),
        "peer_wq": nrm(ks[12], (DEPTH_2, D, PEER_HEADS * PEER_QUERY_DIM), D ** -0.5),
        "peer_keys": nrm(ks[13], (DEPTH_2, PEER_HEADS, 2, PEER_N_KEYS, PEER_HALF), PEER_HALF ** -0.5),
        "peer_u": nrm(ks[14], (DEPTH_2, PEER_N_EXPERTS, D), D ** -0.5),
        "peer_v": nrm(ks[15], (DEPTH_2, PEER_N_EXPERTS, D), 0.25),
    }

def second_block(x, meta_tokens, norm_mix, norm_ffn, pool_w, pool_scale, kv_norm, w_kv, k_norm,
              w_q, q_norm, w_o, peer_wq, peer_keys, peer_u, peer_v):
    B = x.shape[0]
    meta = jnp.broadcast_to(meta_tokens[None].astype(x.dtype), (B, N_META, D_MODEL))
    h = jnp.concatenate([meta, x], axis=1)
    L = h.shape[1]
    k_sh = None
    v_sh = None
    for layer in range(DEPTH_2):
        hn = rmsnorm(h, norm_mix[layer])
        if layer < N_A_LAYERS:
            mix = pool_mixer(hn, pool_w[layer], pool_scale[layer])
        else:
            j = layer - N_A_LAYERS
            q = jnp.einsum('bld,de->ble', hn, w_q[j]).reshape(B, L, SB_HEADS, SB_HEAD_DIM)
            q = rmsnorm(q, q_norm[j])
            mix = jnp.einsum('ble,ed->bld', stick_breaking(q, k_sh, v_sh), w_o[j])
        h = h + mix
        h = h + peer(rmsnorm(h, norm_ffn[layer]), peer_wq[layer], peer_keys[layer],
                     peer_u[layer], peer_v[layer])
        if layer == N_A_LAYERS - 1:
            kv = jnp.einsum('bld,de->ble', rmsnorm(h, kv_norm), w_kv)
            k_sh = rmsnorm(kv[..., :D_MODEL].reshape(B, L, SB_HEADS, SB_HEAD_DIM), k_norm)
            v_sh = kv[..., D_MODEL:].reshape(B, L, SB_HEADS, SB_HEAD_DIM)
    return h[:, N_META:]


def setup_inputs(seed=0):
    out = dict(first_inputs(seed))
    for name, value in second_inputs(seed + 1).items():
        if name != "x":
            out[name + "_2"] = value
    return out


def reference(
    x, pre_mix_g, w_in, conf_dw_w, conf_dw_b, conf_gn_g, conf_gn_b, sconv_w, lru_conv_w,
    lru_conv_b, lru_wa, lru_ba, lru_wx, lru_bx, lru_lam, w_out, post_mix_g, pre_mlp_g, mlp_w1,
    mlp_w2, post_mlp_g, meta_tokens_2, norm_mix_2, norm_ffn_2, pool_w_2, pool_scale_2,
    kv_norm_2, w_kv_2, k_norm_2, w_q_2, q_norm_2, w_o_2, peer_wq_2, peer_keys_2, peer_u_2,
    peer_v_2,
):
    x = first_block(
        x, pre_mix_g, w_in, conf_dw_w, conf_dw_b, conf_gn_g, conf_gn_b, sconv_w, lru_conv_w,
        lru_conv_b, lru_wa, lru_ba, lru_wx, lru_bx, lru_lam, w_out, post_mix_g, pre_mlp_g,
        mlp_w1, mlp_w2, post_mlp_g,
    )
    return second_block(
        x, meta_tokens_2, norm_mix_2, norm_ffn_2, pool_w_2, pool_scale_2, kv_norm_2, w_kv_2,
        k_norm_2, w_q_2, q_norm_2, w_o_2, peer_wq_2, peer_keys_2, peer_u_2, peer_v_2,
    )


_drawn_inputs = setup_inputs


def setup_inputs(seed=0):
    import zlib

    import numpy as np

    out = dict(_drawn_inputs(seed))
    spreads = {}
    factors = {'conf_dw_b': 2.699,
     'conf_gn_b': 4.446,
     'lru_ba': 8.0,
     'lru_bx': 8.0,
     'norm_mix_2': 6.02,
     'norm_ffn_2': 3.685,
     'kv_norm_2': 6.039,
     'k_norm_2': 8.0,
     'q_norm_2': 8.0}
    for name, (base, spread) in spreads.items():
        noise = np.random.default_rng([zlib.crc32(name.encode()), seed]).standard_normal(out[name].shape)
        drawn = base * np.exp(spread * noise) if base else spread * noise
        out[name] = __import__('jax').numpy.asarray(drawn.astype(out[name].dtype))
    for name, factor in factors.items():
        out[name] = (out[name] * factor).astype(out[name].dtype)
    return out
```

```python
import math
from contextlib import ExitStack

import concourse.bass as bass
from concourse import mybir

F32, BF16 = mybir.dt.float32, mybir.dt.bfloat16
I32, U32 = mybir.dt.int32, mybir.dt.uint32
ALU = mybir.AluOpType
ACT = mybir.ActivationFunctionType
X = mybir.AxisListType.X

P = 128
BANK = 512
D = 1024
KD = D // P
T = 256
NT = T // P
META = 16
L = META + T
GW = 256
NC = GW // P
DFF = 4096
CHUNK = 512
FT = CHUNK // P
CONF_K, SC_K, LRU_K = 31, 3, 4
ATT_H, HD = 4, 64
LRU_C = 8.0
EPS, GN_EPS = 1e-6, 1e-5
SB_H = 16
PH, KEYS, TOPK = 8, 128, 16
EXPERTS = KEYS * KEYS
RING = 8
DIAGS = 4
NEG = -1.0e30
MASKED = -3.0e38
POOL_GROUPS = 4

V_CONF = 0
V_SC = V_CONF + CONF_K * NC
V_LRUW = V_SC + SC_K * NC
V_DWB = V_LRUW + LRU_K * NC
V_GNG, V_GNB, V_LRUB, V_BA, V_BX, V_LAM = (V_DWB + NC * i for i in range(1, 7))
V_CHAN = V_LAM + NC
G_PREMIX, G_PREMLP, G_MIX0, G_KV, G_MIX1 = (V_CHAN + KD * i for i in range(5))
V_GAIN = 5 * KD
V_K = V_CHAN + V_GAIN
V_Q = V_K + 1
VECS = V_Q + 1


def program(nc, x, pre_mix_g, w_in, conf_dw_w, conf_dw_b, conf_gn_g, conf_gn_b, sconv_w, lru_conv_w,
            lru_conv_b, lru_wa, lru_ba, lru_wx, lru_bx, lru_lam, w_out, post_mix_g, pre_mlp_g, mlp_w1,
            mlp_w2, post_mlp_g, meta_tokens, norm_mix, norm_ffn, pool_w, pool_scale, kv_norm, w_kv,
            k_norm, w_q, q_norm, w_o, peer_wq, peer_keys, peer_u, peer_v, out):
    ctx = ExitStack()
    with ctx:
        def sb(name, shape, dt=F32):
            return ctx.enter_context(nc.sbuf_tensor(name, shape, dt))

        named, count = {}, {}

        def S(name):
            if name not in named:
                named[name] = nc.alloc_semaphore(name=name)
                count[name] = 0
            return named[name]

        def forget(kept):
            gone = [name for name in named if name not in kept]
            nc.clear_and_free_semaphores([named.pop(name) for name in gone])
            for name in gone:
                del count[name]
            nc.all_engine_barrier()

        def step(engine, instruction, signals):
            instruction.then_inc(S(signals), 1)
            count[signals] += 1
            engine.wait_ge(S(signals), count[signals])

        big = sb("big", [P, 2 * 16384])
        h = sb("residual", [P, 3, D])
        hn = sb("normed", [P, NT, D])
        ua = sb("ua", [P, 18 * 256])
        sc = sb("sc", [P, 17 * 256])
        gb = sb("gain_rows", [P, 2, D])
        vec = sb("vectors", [P, VECS])
        ident = sb("ident", [P, P])
        group_mean = sb("group_mean", [P, P])
        zeros = sb("zeros", [P, P], BF16)
        rep = sb("rep", [META, PH, META])
        eps_col = sb("eps", [P, 1])
        rept = sb("rept", [P, META])
        stats = sb("stats", [P, 12])
        lam_s = sb("softplus_lam", [P, 6 * NC])
        lam8 = sb("minus_8_softplus", [P, NC])
        att_m = sb("att_m", [P, 2 * ATT_H])
        att_s = sb("att_s", [P, 2 * ATT_H])
        diag = sb("diag", [P, DIAGS, P])
        ratio = sb("ratio", [P, POOL_GROUPS, META])
        ratio_i = sb("ratio_i", [P, META], I32)
        work = sb("work", [P, 3, 256])
        ints = sb("ints", [P, 2, TOPK], I32)
        half_v = sb("half_v", [P, 2, TOPK])
        half_i = sb("half_i", [P, 2, TOPK], U32)
        half_f = sb("half_f", [P, 2, TOPK])
        best = sb("best", [P, 2, TOPK])
        best_at = sb("best_at", [P, TOPK], U32)
        pos_f = sb("pos_f", [P, 2, TOPK])
        picked = sb("picked", [P, 2, TOPK])
        expert = sb("expert", [P, 2, TOPK], U32)
        neg_best = sb("neg_best", [P, 2])
        gate = sb("gate", [P, 2, TOPK])
        gate_sum = sb("gate_sum", [P, 2])
        dots = sb("dots", [P, 2, TOPK])
        weight = sb("weight", [P, 2, TOPK])
        iota16 = sb("iota16", [P, TOPK])
        iota16_i = sb("iota16_i", [P, TOPK], I32)
        ps = ctx.enter_context(nc.psum_tensor("ps", [P, 8 * BANK], F32))

        def bank(b, n=1):
            return ps[:, BANK * b:BANK * (b + n)]

        def cut(ap, lo, a, b):
            return ap[:, lo:lo + a * b].rearrange("p (a b) -> p a b", a=a)

        win = [cut(big, 4096 * c, KD, CHUNK) for c in range(5)]
        wout = cut(big, 5 * 4096, KD, D)
        tail = 28672
        alibi = cut(big, tail, ATT_H, 384)
        soft = cut(big, tail + 1536, ATT_H, 384)
        bd = big[:, tail + 3072:tail + 3584].rearrange("p (w c n) -> p w c n", w=2, c=NC)
        alibi_i = big[:, tail + 3584:tail + 3968].bitcast(I32)
        probs_t = cut(big, 0, ATT_H, 384)
        r_s, i_s, a_s, th_s, b_s = (cut(big, 1536 + 512 * i, NC, T) for i in range(5))
        sg, ub, uc, uq, uk, uv, gg, xc, gd = (cut(ua, 512 * i, NC, T) for i in range(9))
        zpad = cut(sc, 0, NC, CONF_K - 1 + T)
        spad = cut(sc, 572, NC, SC_K - 1 + T)
        xpad = cut(sc, 1088, NC, LRU_K - 1 + T)
        conv = cut(sc, 1606, NC, T)
        ht = cut(sc, 2118, KD, T)
        yt = hn[:, :, :].rearrange("p t (a n) -> p (t a) n", n=T)
        tmp_m = sc[0:META, 2048:3072]
        tmp = sc[:, 0:2048].rearrange("p (t n) -> p t n", t=NT)
        lam = [lam_s[:, NC * i:NC * (i + 1)] for i in range(6)]
        vrows = gb[:, 1, 0:P]
        grows = gb[:, 1, P:2 * P]
        w1b = [cut(big, 4096, KD, CHUNK), cut(big, 8192, KD, CHUNK)]
        w2b = [cut(big, 12288, FT, D), cut(big, 0, FT, D)]
        h2t = cut(ua, 0, KD, T)
        relu = cut(sc, 0, 2, T)
        act2 = cut(sc, 512, 4, T)
        PADL = META + L
        keys_in = [cut(big, 12672, 2 * PH, KEYS), cut(sc, 2048, 2 * PH, KEYS)]
        keys_t = cut(big, 2304, 2 * PH, KEYS)
        q_meta = big[:, 4608:6656].rearrange("p (w h n) -> p w h n", w=2, h=PH)
        seq = [cut(big, PADL * KD * i, KD, PADL) for i in range(3)]
        hnt = cut(big, 0, KD, L)
        pooled = cut(big, 7168, KD, L)
        hnm = big[0:META, 9600:9600 + D]
        poolw = cut(big, 10624, 2 * POOL_GROUPS, GW)
        qt = cut(ua, 0, 2 * PH, L)
        scores = cut(sc, 0, 2 * PH + 1, 256)
        W = 16384
        wq_peer = cut(big, W, KD, 2 * D)
        wkv = cut(big, W, KD, 2 * D)
        wq_att = cut(big, 0, KD, D)
        wo_att = cut(big, 8192, KD, D)
        kv_in, q_in = cut(sc, 0, KD, L), cut(sc, KD * L, KD, T)
        k_t, q_t = cut(ua, 0, KD, L), cut(ua, KD * L, KD, T)
        v_meta = gb[0:META, 1, :]
        Z = META + P + L
        zs, ls, ws = (cut(big, 4 * Z * i, 4, Z) for i in range(3))
        wt = cut(big, 12 * Z, 2, 3 * P)
        wt_meta = cut(big, 12 * Z + 768, 2, T)
        k_now = cut(big, 12 * Z + 1280, 2, L)
        q_now = cut(big, 12 * Z + 1824, 2, T)
        v_now = big[:, 12 * Z + 2336:12 * Z + 3104].rearrange("p (a t n) -> p a t n", a=2, t=3)
        neg_mask = diag[:, :, :].rearrange("p a n -> p (a n)")[:, 0:Z]
        seg = work[:, :, :].rearrange("p a n -> p (a n)")[:, 0:Z]
        att_y = cut(sc, 0, KD, T)
        ring_u = [big[:, D * i:D * (i + 1)] for i in range(RING)]
        ring_v = [big[:, 8192 + D * i:8192 + D * (i + 1)] for i in range(RING)]

        X_TILES = [(P, t, META + P * t) for t in range(NT)]
        META_TILE = (META, NT, 0)

        def normed(t, tag="ffn0"):
            return (v_meta if tag == "kv" else hnm) if t == NT else hn[:, t, :]

        def tile_banks(t):
            return bank(4, 2)[0:META] if t == NT else bank(2 * t, 2)

        def passed(engine):
            engine.sem_inc(S("waits_passed"), 1)

        def act_squares(act, tiles, after, tag):
            for n, (rows, t, _) in enumerate(tiles):
                if after:
                    act.wait_ge(S(after), n + 1)
                step(act, nc.scalar.activation(ua[0:rows, 0:D], h[0:rows, t, :], ACT.Square,
                                               accum_out=stats[0:rows, t:t + 1]), tag + "_squares")
            act.wait_ge(S(tag + "_var"), 1)
            step(act, nc.scalar.activation(stats[:, 6:9], stats[:, 3:6], ACT.Sqrt), tag + "_std")

        def dve_inverse_rms(dve, tiles, tag):
            dve.wait_ge(S(tag + "_squares"), len(tiles))
            step(dve, nc.vector.tensor_scalar(stats[:, 3:6], stats[:, 0:3], 1.0 / D, EPS, ALU.mult, ALU.add),
                 tag + "_var")
            dve.wait_ge(S(tag + "_std"), 1)
            step(dve, nc.vector.reciprocal(stats[:, 9:12], stats[:, 6:9]), tag + "_inverse")

        def pe_transposes(pe, tiles, tag):
            for n, (rows, t, _) in enumerate(tiles):
                pe.wait_ge(S(tag + "_normed"), n + 1)
                for k in range(KD):
                    to = bank(4)[:, META * k:META * (k + 1)] if t == NT else \
                        bank(2 * t + k // 4)[:, P * (k % 4):P * (k % 4 + 1)]
                    last = nc.tensor.transpose(to, normed(t, tag)[0:rows, P * k:P * (k + 1)], ident[0:rows, 0:rows])
                last.then_inc(S(tag + "_t"), 1)

        def transposed(tiles):
            for n, (rows, t, at) in enumerate(tiles):
                if t == NT:
                    yield n, cut(bank(4), 0, KD, META), 0, KD, at, META
                else:
                    for j in range(2):
                        yield n, cut(bank(2 * t + j), 0, 4, P), 4 * j, 4, at, P

        def peer_norm_dve(dve, tiles, tag, gains, gains_loaded):
            v = nc.vector
            dve_inverse_rms(dve, tiles, tag)
            dve.wait_ge(S(gains_loaded), 16 * (2 if gains_loaded == "gain1_loaded" else 3))
            for rows, t, _ in tiles:
                step(dve, v.scalar_tensor_tensor(normed(t)[0:rows], h[0:rows, t, :], stats[0:rows, 9 + t:10 + t],
                                                 gains[0:rows], ALU.mult, ALU.mult), tag + "_normed")
            for n, psum, k, blocks, at, cols in transposed(tiles):
                dve.wait_ge(S(tag + "_t"), n + 1)
                step(dve, v.tensor_copy(hnt[:, k:k + blocks, at:at + cols], psum), tag + "_t_out")

        def peer_scores_pe(pe, tiles, layer, tag):
            m = nc.tensor
            width = sum(r for r, _, _ in tiles)
            c0 = L - width
            pe.wait_ge(S(f"peer_wq{layer}_loaded"), 16)
            pe.wait_ge(S(tag + "_t_out"), sum(1 for _ in transposed(tiles)))
            for hp in range(2 * PH):
                if hp >= 3:
                    pe.wait_ge(S(tag + "_q_out"), hp - 2)
                for k in range(KD):
                    last = m.matmul(bank(5 + hp % 3)[:, 0:width], wq_peer[:, k, P * hp:P * (hp + 1)], hnt[:, k, c0:L],
                                    start=(k == 0), stop=(k == KD - 1))
                last.then_inc(S(tag + "_q_done"), 1)
                if hp == 0:
                    pe.wait_ge(S(f"peer_keys{layer}_loaded"), 16)
                    for j in range(2 * PH):
                        last = m.transpose(bank(j // 4)[:, P * (j % 4):P * (j % 4 + 1)], keys_in[layer][:, j, :], ident[:])
                        if j % 4 == 3:
                            last.then_inc(S(tag + "_keys_t"), 1)
            pe.wait_ge(S(tag + "_q_out"), 2 * PH)
            pe.wait_ge(S(tag + "_keys_out"), 4)
            for pair in range(NT * PH // 2):
                if pair >= 4:
                    pe.wait_ge(S(tag + "_scores_out"), pair - 3)
                for u in (2 * pair, 2 * pair + 1):
                    for p in range(2):
                        hp, at = 2 * (u % PH) + p, META + P * (u // PH)
                        last = m.matmul(bank(pair % 4)[:, 256 * (u % 2) + P * p:256 * (u % 2) + P * (p + 1)],
                                        qt[:, hp, at:at + P], keys_t[:, hp, :], start=True, stop=True)
                last.then_inc(S(tag + "_scores_done"), 1)
            if layer == 0:
                pe.wait_ge(S("q_meta_ready"), 1)
                for p in range(2):
                    for head in range(PH):
                        last = m.matmul(bank(4)[:, P * p:P * (p + 1)], q_meta[:, p, head, :], keys_t[:, 2 * head + p, :],
                                        start=(head == 0), stop=(head == PH - 1))
                last.then_inc(S(tag + "_scores_done"), 1)
                for half in range(2):
                    m.matmul(bank(6 + half), rep[:, :, :].rearrange("p h t -> p (h t)"),
                             hnm[:, BANK * half:BANK * (half + 1)], start=True, stop=True).then_inc(S("meta_rows"), 1)

        def peer_queries_act(act, tiles, tag):
            c0 = L - sum(r for r, _, _ in tiles)
            for hp in range(2 * PH):
                act.wait_ge(S(tag + "_q_done"), hp + 1)
                step(act, nc.scalar.activation(qt[:, hp, c0:L], bank(5 + hp % 3)[:, 0:L - c0], ACT.Copy), tag + "_q_out")

        def peer_scores_dve(dve, layer, tag):
            v = nc.vector
            for j in range(4):
                dve.wait_ge(S(tag + "_keys_t"), j + 1)
                step(dve, v.tensor_copy(keys_t[:, 4 * j:4 * j + 4, :], cut(bank(j), 0, 4, P)), tag + "_keys_out")
            if layer == 0:
                dve.wait_ge(S(tag + "_q_out"), 2 * PH)
                step(dve, v.memset(q_meta, 0.0), "dve_order")
                for head in range(PH):
                    ins = v.tensor_copy(q_meta[:, :, head, META * head:META * (head + 1)],
                                        qt[:, 2 * head:2 * head + 2, 0:META])
                    step(dve, ins, "q_meta_ready" if head == PH - 1 else "dve_order")
            for pair in range(NT * PH // 2):
                dve.wait_ge(S(tag + "_scores_done"), pair + 1)
                step(dve, v.tensor_copy(scores[:, 2 * pair:2 * pair + 2, :], cut(bank(pair % 4), 0, 2, 256)),
                     tag + "_scores_out")
            if layer == 0:
                dve.wait_ge(S(tag + "_scores_done"), NT * PH // 2 + 1)
                step(dve, v.tensor_copy(scores[:, NT * PH, :], bank(4)[:, 0:256]), tag + "_scores_out")

        def route(dve, layer, u, par):
            v = nc.vector
            w0, w1, w2 = (work[:, i, :] for i in range(3))

            def done(instruction):
                dve.drain()

            def top16(values, at, source, rest):
                done(v.max(values[:, 0:8], source))
                done(v.max_index(at[:, 0:8], values[:, 0:8], source))
                done(v.match_replace(rest, values[:, 0:8], source, MASKED))
                done(v.max(values[:, 8:16], rest))
                done(v.max_index(at[:, 8:16], values[:, 8:16], rest))

            done(v.tensor_copy(w0.unsqueeze(1), scores[:, bass.ds(u, 1), :]))
            for p in range(2):
                top16(half_v[:, p, :], half_i[:, p, :], w0[:, P * p:P * (p + 1)], w1[:, P * p:P * (p + 1)])
            v.tensor_scalar(half_f[:, 0, :], half_i[:, 0, :], float(KEYS), float(layer * EXPERTS), ALU.mult, ALU.add)
            v.tensor_copy(half_f[:, 1, :], half_i[:, 1, :])
            square = [P, TOPK, TOPK]
            sums = w2.rearrange("p (i j) -> p i j", i=TOPK)
            done(v.tensor_tensor(sums, half_v[:, 0, :].unsqueeze(2).broadcast_to(square),
                                 half_v[:, 1, :].unsqueeze(1).broadcast_to(square), ALU.add))
            top16(best[:, par, :], best_at[:], w2, w0)
            v.tensor_scalar(neg_best[:, par:par + 1], best[:, par, 0:1], -1.0, None, ALU.mult)\
                .then_inc(S(f"best_ready{layer}"), 1)
            v.tensor_scalar(ints[:, 0, :], best_at[:].bitcast(I32), 4, None, ALU.logical_shift_right)
            done(v.tensor_scalar(ints[:, 1, :], best_at[:].bitcast(I32), TOPK - 1, None, ALU.bitwise_and))
            done(v.tensor_copy(pos_f[:], ints[:]))
            for p, w in enumerate((w0, w1)):
                onehot = w.rearrange("p (i j) -> p i j", i=TOPK)
                done(v.tensor_tensor(onehot, pos_f[:, p, :].unsqueeze(2).broadcast_to(square),
                                     iota16[:].unsqueeze(1).broadcast_to(square), ALU.is_equal))
                done(v.tensor_tensor(onehot, onehot, half_f[:, p, :].unsqueeze(1).broadcast_to(square), ALU.mult))
                done(v.tensor_reduce(picked[:, p, :], onehot, X, ALU.add))
            done(v.tensor_tensor(expert[:, par, :], picked[:, 0, :], picked[:, 1, :], ALU.add)
                 .then_inc(S(f"experts_ready{layer}"), 1))

        def gathers(pool, layer, u, par):
            tables = (("u", ring_u, peer_u, "dots_done"), ("v", ring_v, peer_v, "v_used"))
            pool.wait_ge(S(f"experts_ready{layer}"), u + 1)
            passed(pool)
            for name, ring, table, freed in tables:
                rows = table.rearrange("l e d -> (l e) d")
                for k in range(TOPK):
                    pool.wait_ge(S(f"{freed}{layer}"), u * TOPK + (k + 1))
                    passed(pool)
                    nc.gpsimd.indirect_dma_start(
                        out=ring[k % RING], out_offset=None, in_=rows,
                        in_offset=bass.IndirectOffsetOnAxis(ap=expert[:, par, k:k + 1], axis=0))\
                        .then_inc(S(f"{name}{k % RING}_loaded{layer}"), 16)

        def unit_dots(dve, layer, u, par, rows):
            v = nc.vector
            for k in range(TOPK):
                dve.wait_ge(S(f"u{k % RING}_loaded{layer}"), u * 32 + 16 * (k // RING + 1))
                v.tensor_tensor_reduce(out=ring_u[k % RING], in0=ring_u[k % RING], in1=rows, scale=1.0, scalar=0.0,
                                       op0=ALU.mult, op1=ALU.add, accum_out=dots[:, par, k:k + 1])\
                    .then_inc(S(f"dots_done{layer}"), 1)
            dve.wait_ge(S(f"gelu_done{layer}"), u + 1)
            v.reciprocal(gate_sum[:, par:par + 1], gate_sum[:, par:par + 1])
            dve.drain()
            v.scalar_tensor_tensor(weight[:, par, :], dots[:, par, :], gate_sum[:, par:par + 1], gate[:, par, :],
                                   ALU.mult, ALU.mult).then_inc(S(f"weights_ready{layer}"), 1)

        def unit_act(act, layer, u, par, base, cols):
            a = nc.scalar
            act.wait_ge(S(f"best_ready{layer}"), u + 1)
            a.activation(gate[:, par, :], best[:, par, :], ACT.Exp, bias=neg_best[:, par:par + 1],
                         accum_out=gate_sum[:, par:par + 1])
            act.wait_ge(S(f"dots_done{layer}"), u * TOPK + (RING + TOPK))
            a.activation(dots[:, par, :], dots[:, par, :], ACT.Gelu).then_inc(S(f"gelu_done{layer}"), 1)
            act.wait_ge(S(f"weights_ready{layer}"), u + 1)
            for k in range(TOPK):
                act.wait_ge(S(f"v_used{layer}"), u * TOPK + (k + 1 + RING - DIAGS))
                a.activation(diag[:, k % DIAGS, 0:cols], base, ACT.Copy, scale=weight[:, par, k:k + 1])\
                    .then_inc(S(f"diag_ready{layer}"), 1)

        def unit_pe(pe, layer, u, y, cols):
            for k in range(TOPK):
                pe.wait_ge(S(f"v{k % RING}_loaded{layer}"), u * 32 + 16 * (k // RING + 1))
                pe.wait_ge(S(f"diag_ready{layer}"), u * TOPK + (k + 1))
                for half in range(2):
                    last = nc.tensor.matmul(y[:, BANK * half:BANK * (half + 1)], diag[:, k % DIAGS, 0:cols],
                                            ring_v[k % RING][:, BANK * half:BANK * (half + 1)], start=False, stop=False)
                last.then_inc(S(f"v_used{layer}"), 1)

        META_UNIT = NT * PH
        y_x, rows_x, y_m, rows_m = bank(0, 2), bank(2, 2), bank(4, 2)[0:META], bank(6, 2)

        def peer_gpsimd(pool, layer):
            with pool.Fori(0, NT) as tile:
                with pool.Fori(0, PH // 2) as pair:
                    for par in range(2):
                        gathers(pool, layer, tile * PH + pair * 2 + par, par)
            if layer == 0:
                gathers(pool, layer, META_UNIT, 0)

        def peer_vector(dve, layer):
            dve.sem_inc(S(f"dots_done{layer}"), RING)
            route(dve, layer, 0, 0)
            with dve.Fori(0, NT) as tile:
                dve.wait_ge(S(f"rows_ready{layer}"), tile + 1)
                passed(dve)
                with dve.Fori(0, PH // 2) as pair:
                    for par in range(2):
                        u = tile * PH + pair * 2 + par
                        unit_dots(dve, layer, u, par, rows_x)
                        dve.wait_ge(S(f"v_used{layer}"), u * TOPK + RING)
                        passed(dve)
                        route(dve, layer, u + 1, 1 - par)
            if layer == 0:
                unit_dots(dve, layer, META_UNIT, 0, rows_m)

        def peer_scalar(act, layer):
            a = nc.scalar
            act.sem_inc(S(f"tile_out{layer}"), 1)
            with act.Fori(0, NT) as tile:
                act.wait_ge(S(f"dots_done{layer}"), tile * (PH * TOPK) + RING)
                passed(act)
                a.activation(rows_x.unsqueeze(1), hn[:, bass.ds(tile, 1), :], ACT.Copy)\
                    .then_inc(S(f"rows_ready{layer}"), 1)
                with act.Fori(0, PH // 2) as pair:
                    for par in range(2):
                        unit_act(act, layer, tile * PH + pair * 2 + par, par, ident[:], P)
                act.wait_ge(S(f"y_closed{layer}"), tile + 1)
                passed(act)
                a.activation(h[:, bass.ds(tile, 1), :], y_x.unsqueeze(1), ACT.Copy).then_inc(S(f"tile_out{layer}"), 1)
            if layer == 0:
                unit_act(act, layer, META_UNIT, 0, rept[:], META)
                act.wait_ge(S(f"y_closed{layer}"), NT + 1)
                a.activation(h[0:META, NT, :], y_m, ACT.Copy).then_inc(S(f"tile_out{layer}"), 1)

        def peer_tensor(pe, layer):
            m = nc.tensor
            pe.sem_inc(S(f"v_used{layer}"), RING)

            def close(y, cols):
                for half in range(2):
                    last = m.matmul(y[:, BANK * half:BANK * (half + 1)].rearrange("p (a n) -> p a n", a=4),
                                    zeros[:, 0:cols], zeros[:].unsqueeze(1).broadcast_to([P, 4, P]),
                                    start=False, stop=True)
                last.then_inc(S(f"y_closed{layer}"), 1)

            with pe.Fori(0, NT) as tile:
                pe.wait_ge(S(f"tile_out{layer}"), tile + 1)
                for half in range(2):
                    m.matmul(y_x[:, BANK * half:BANK * (half + 1)].unsqueeze(1), ident[:],
                             h[:, bass.ds(tile, 1), BANK * half:BANK * (half + 1)], start=True, stop=False)
                with pe.Fori(0, PH // 2) as pair:
                    for par in range(2):
                        unit_pe(pe, layer, tile * PH + pair * 2 + par, y_x, P)
                close(y_x, P)
            if layer == 0:
                for half in range(2):
                    m.matmul(y_m[:, BANK * half:BANK * (half + 1)], ident[0:META, 0:META],
                             h[0:META, NT, BANK * half:BANK * (half + 1)], start=True, stop=False)
                unit_pe(pe, layer, META_UNIT, y_m, META)
                close(y_m, META)

        with nc.Block(no_gpsimd_drain=True) as block:
            @block.sync
            def _(sp):
                sp.dma_start(h[:, 0:NT, :], x[0].rearrange("(t p) d -> p t d", p=P)).then_inc(S("x_loaded"), 16)
                rows = [(conf_dw_w[0], CONF_K), (sconv_w[0], SC_K), (lru_conv_w[0], LRU_K), (conf_dw_b, 1),
                        (conf_gn_g, 1), (conf_gn_b, 1), (lru_conv_b, 1), (lru_ba, 1), (lru_bx, 1), (lru_lam, 1)]
                at = 0
                for v, n in rows:
                    sp.dma_start(vrows[at:at + n * NC, :], v.rearrange("k (c p) -> (k c) p", p=P))\
                        .then_inc(S("vectors_loaded"), 16)
                    at += n * NC
                gains = [pre_mix_g, pre_mlp_g, norm_mix[0:1], kv_norm.rearrange("(o n) -> o n", o=1), norm_mix[1:2]]
                for i, v in enumerate(gains):
                    sp.dma_start(grows[KD * i:KD * (i + 1), :], v.rearrange("o (k p) -> (o k) p", p=P))\
                        .then_inc(S("vectors_loaded"), 16)
                k_row = k_norm.rearrange("(o n) -> o n", o=1)
                for i, v in enumerate((k_row, q_norm)):
                    for half in range(2):
                        sp.dma_start(grows[V_GAIN + i:V_GAIN + i + 1, HD * half:HD * (half + 1)], v)\
                            .then_inc(S("vectors_loaded"), 16)
                w_in_v = w_in[0].rearrange("(k p) n -> p k n", p=P)
                for c in range(5):
                    sp.dma_start(win[c], w_in_v[:, :, CHUNK * c:CHUNK * (c + 1)]).then_inc(S(f"w_in{c}_loaded"), 16)
                sp.wait_ge(S("constants_ready"), 8)
                for w, blocks in enumerate((lru_wa, lru_wx)):
                    for g in range(2 * NC):
                        r = HD * (g % 2)
                        sp.dma_start(bd[r:r + HD, w, g // 2, r:r + HD], blocks[0, g]).then_inc(S("lru_w_loaded"), 16)
                sp.dma_start(wout, w_out[0].rearrange("(k p) n -> p k n", p=P)).then_inc(S("w_out_loaded"), 16)
                sp.dma_start(gb[:, 0, :], post_mix_g[0].partition_broadcast(P)).then_inc(S("gain0_loaded"), 16)
                sp.dma_start(h[0:META, NT, :], meta_tokens).then_inc(S("meta_loaded"), 16)
                sp.wait_ge(S("u_done"), 10)
                w1_v = mlp_w1[0].rearrange("(k p) n -> p k n", p=P)
                w2_v = mlp_w2[0].rearrange("(f p) n -> p f n", p=P)
                for c in range(2):
                    sp.dma_start(w1b[c], w1_v[:, :, CHUNK * c:CHUNK * (c + 1)]).then_inc(S(f"w1_{c}_loaded"), 16)
                sp.dma_start(w2b[0], w2_v[:, 0:FT, :]).then_inc(S("w2_0_loaded"), 16)
                sp.wait_ge(S("vectors_t"), 1)
                sp.dma_start(gb[:, 1, :], post_mlp_g[0].partition_broadcast(P)).then_inc(S("gain1_loaded"), 16)

            @block.gpsimd
            def _(pool):
                g = nc.gpsimd

                def const(instruction):
                    step(pool, instruction, "constants_ready")

                const(g.memset(ident[:], 0.0))
                const(g.affine_select(out=ident[:], in_=ident[:], compare_op=ALU.not_equal, fill=1.0, base=0,
                                      pattern=[[-1, P]], channel_multiplier=1))
                const(g.memset(zpad[:, :, 0:CONF_K - 1], 0.0))
                const(g.memset(spad[:, :, 0:SC_K - 1], 0.0))
                const(g.memset(xpad[:, :, 0:LRU_K - 1], 0.0))
                const(g.memset(zeros[:], 0.0))
                const(g.memset(group_mean[:], 0.0))
                const(g.memset(bd, 0.0))
                for i in range(2):
                    const(g.memset(group_mean[HD * i:HD * (i + 1), HD * i:HD * (i + 1)], 1.0 / HD))
                const(g.iota(alibi_i[:, 0:P], [[-1, P]], base=0, channel_multiplier=1))
                const(g.iota(alibi_i[:, P:384], [[-1, T]], base=P, channel_multiplier=1))
                for a in range(ATT_H):
                    const(g.tensor_copy(alibi[:, a, :], alibi_i))
                    const(g.tensor_scalar(alibi[:, a, :], alibi[:, a, :], -(2.0 ** (-8.0 * (a + 1) / ATT_H)), None,
                                          ALU.mult))
                    for lo, n, base in ((0, P, 0), (P, T, P)):
                        const(g.affine_select(out=alibi[:, a, lo:lo + n], in_=alibi[:, a, lo:lo + n],
                                              compare_op=ALU.is_ge, fill=NEG, base=base, pattern=[[-1, n]],
                                              channel_multiplier=1))
                const(g.iota(ratio_i[:], [[1, META]], base=1, channel_multiplier=0))
                const(g.iota(iota16_i[:], [[1, TOPK]], base=0, channel_multiplier=0))
                const(g.memset(rep[:], 0.0))
                const(g.affine_select(out=rep[:], in_=rep[:], compare_op=ALU.not_equal, fill=1.0, base=0,
                                      pattern=[[0, PH], [-1, META]], channel_multiplier=1))

            @block.scalar
            def _(act):
                a = nc.scalar

                act.wait_ge(S("x_loaded"), 16)
                for t in range(NT):
                    step(act, a.activation(ua[:, 0:D], h[:, t, :], ACT.Square, accum_out=stats[:, t:t + 1]), "x_squares")
                act.wait_ge(S("x_var"), 1)
                step(act, a.activation(stats[:, 4:6], stats[:, 2:4], ACT.Sqrt), "x_std")
                act.wait_ge(S("lam_abs"), 1)
                step(act, a.activation(lam[3], lam[1], ACT.Exp, scale=-1.0), "lam_exp")
                act.wait_ge(S("lam_one"), 1)
                step(act, a.activation(lam[5], lam[4], ACT.Ln), "lam_ln")
                act.wait_ge(S("u_done"), 2)
                step(act, a.activation(sg, cut(bank(5), 0, NC, T), ACT.Sigmoid), "u_out")
                for pair, b, to in ((2, 6, ub), (3, 7, uc), (5, 1, uq), (6, 2, uk), (7, 3, uv)):
                    act.wait_ge(S("u_done"), pair + 1)
                    step(act, a.activation(to, cut(bank(b), 0, NC, T), ACT.Copy), "u_out")
                act.wait_ge(S("u_done"), 9)
                act.wait_ge(S("constants_ready"), 5)
                step(act, a.activation(xpad[:, :, LRU_K - 1:], cut(bank(6), 0, NC, T), ACT.Copy), "u_out")
                act.wait_ge(S("gn_var"), 1)
                step(act, a.activation(uc, sg, ACT.Sqrt), "gn_std")
                act.wait_ge(S("u_done"), 10)
                step(act, a.activation(gg, cut(bank(7), 0, NC, T), ACT.Gelu_apprx_tanh), "u_out")
                for head in range(ATT_H):
                    act.wait_ge(S("att_max"), 2 * head + 2)
                    for t, (lo, n) in enumerate(((0, P), (P, T))):
                        step(act, a.activation(soft[:, head, lo:lo + n], soft[:, head, lo:lo + n], ACT.Exp,
                                               bias=att_m[:, 2 * head + t:2 * head + t + 1],
                                               accum_out=att_s[:, 2 * head + t:2 * head + t + 1]), "att_exp")
                act.wait_ge(S("lru_gates_done"), 2)
                for w, (to, bias) in enumerate(((r_s, V_BA), (i_s, V_BX))):
                    for c in range(NC):
                        step(act, a.activation(to[:, c], bank(4 + w)[:, T * c:T * (c + 1)], ACT.Sigmoid,
                                               bias=vec[:, bias + c:bias + c + 1]), "lru_sigmoid")
                act.wait_ge(S("gn_out"), NC)
                step(act, a.activation(yt[:, 0:NC], gd, ACT.Silu), "y_a")
                act.wait_ge(S("lru_log"), NC)
                step(act, a.activation(a_s, r_s, ACT.Exp), "lru_a")
                step(act, a.activation(th_s, r_s, ACT.Tanh, scale=-1.0), "lru_a")
                act.wait_ge(S("lru_sq"), 1)
                step(act, a.activation(th_s, th_s, ACT.Sqrt), "lru_mult")
                act.wait_ge(S("att_pv"), 1)
                step(act, a.activation(yt[:, 4:6], cut(bank(6), 0, NC, T), ACT.Copy), "y_c")
                act.wait_ge(S("y_done"), 1)
                for t in range(NT):
                    step(act, a.activation(ua[:, 0:D], bank(2 * t, 2), ACT.Square, accum_out=stats[:, t:t + 1]), "y_squares")
                act.wait_ge(S("y_var"), 1)
                step(act, a.activation(stats[:, 4:6], stats[:, 2:4], ACT.Sqrt), "y_std")
                for t in range(NT):
                    act.wait_ge(S("x1"), t + 1)
                    step(act, a.activation(ua[:, 0:D], h[:, t, :], ACT.Square, accum_out=stats[:, t:t + 1]), "x1_squares")
                act.wait_ge(S("x1_var"), 1)
                step(act, a.activation(stats[:, 4:6], stats[:, 2:4], ACT.Sqrt), "x1_std")

            @block.vector
            def _(dve):
                v = nc.vector

                def chain(instruction):
                    step(dve, instruction, "dve_order")

                def rms(squares, var, std):
                    dve.wait_ge(S(squares), NT)
                    step(dve, v.tensor_scalar(stats[:, 2:4], stats[:, 0:2], 1.0 / D, EPS, ALU.mult, ALU.add), var)
                    dve.wait_ge(S(std), 1)
                    chain(v.reciprocal(stats[:, 6:8], stats[:, 4:6]))

                rms("x_squares", "x_var", "x_std")
                for t in range(NT):
                    step(dve, v.tensor_scalar(hn[:, t, :], h[:, t, :], stats[:, 6 + t:7 + t], None, ALU.mult), "x_normed")
                dve.wait_ge(S("vectors_t"), 1)
                chain(v.tensor_copy(vec[:, 0:V_CHAN], bank(7)[:, 0:V_CHAN]))
                step(dve, v.tensor_copy(vec[:, V_CHAN:VECS], bank(7)[:, P:P + VECS - V_CHAN]), "vectors_ready")
                for t in range(NT):
                    dve.wait_ge(S("x_t"), t + 1)
                    for j in range(2):
                        gain = vec[:, G_PREMIX + 4 * j:G_PREMIX + 4 * j + 4].unsqueeze(2).broadcast_to([P, 4, P])
                        step(dve, v.tensor_tensor(ht[:, 4 * j:4 * j + 4, P * t:P * (t + 1)],
                                                  cut(bank(2 * t + j), 0, 4, P), gain, ALU.mult), "h_t")
                lamv = vec[:, V_LAM:V_LAM + NC]
                chain(v.tensor_scalar(lam[0], lamv, -1.0, 0.0, ALU.mult, ALU.max))
                chain(v.tensor_scalar(lam[1], lamv, -1.0, None, ALU.mult))
                step(dve, v.tensor_tensor(lam[1], lam[1], lamv, ALU.max), "lam_abs")
                dve.wait_ge(S("lam_exp"), 1)
                step(dve, v.tensor_scalar(lam[4], lam[3], 1.0, None, ALU.add), "lam_one")
                chain(v.tensor_scalar(lam[1], lam[4], -1.0, None, ALU.add))
                chain(v.tensor_tensor(lam[1], lam[3], lam[1], ALU.subtract))
                chain(v.reciprocal(lam[2], lam[4]))
                chain(v.tensor_tensor(lam[1], lam[1], lam[2], ALU.mult))
                chain(v.tensor_tensor(lam[0], lam[0], lam[1], ALU.add))
                dve.wait_ge(S("lam_ln"), 1)
                chain(v.tensor_tensor(lam[0], lam[0], lam[5], ALU.add))
                chain(v.tensor_scalar(lam8[:], lam[0], -LRU_C, None, ALU.mult))
                dve.wait_ge(S("u_done"), 1)
                dve.wait_ge(S("u_out"), 1)
                dve.wait_ge(S("constants_ready"), 5)
                chain(v.tensor_tensor(zpad[:, :, CONF_K - 1:], cut(bank(4), 0, NC, T), sg, ALU.mult))
                for c in range(NC):
                    chain(v.tensor_scalar(conv[:, c], zpad[:, c, 0:T], vec[:, V_CONF + c:V_CONF + c + 1],
                                          vec[:, V_DWB + c:V_DWB + c + 1], ALU.mult, ALU.add))
                with dve.Fori(1, CONF_K) as tap:
                    for c in range(NC):
                        v.scalar_tensor_tensor(conv[:, c], zpad[:, c, bass.ds(tap, T)],
                                               vec[:, bass.ds(tap * NC + (V_CONF + c), 1)], conv[:, c],
                                               ALU.mult, ALU.add)
                    dve.drain()
                dve.drain().then_inc(S("conv_done"), 1)
                dve.wait_ge(S("u_done"), 5)
                dve.wait_ge(S("u_out"), 3)
                step(dve, v.tensor_tensor(spad[:, :, SC_K - 1:], cut(bank(0), 0, NC, T), uc, ALU.mult), "xs_used")
                for c in range(NC):
                    chain(v.tensor_scalar(uc[:, c], spad[:, c, 0:T], vec[:, V_SC + c:V_SC + c + 1], None, ALU.mult))
                for tap in range(1, SC_K):
                    for c in range(NC):
                        col = V_SC + tap * NC + c
                        chain(v.scalar_tensor_tensor(uc[:, c], spad[:, c, tap:tap + T], vec[:, col:col + 1], uc[:, c],
                                                     ALU.mult, ALU.add))
                dve.wait_ge(S("gn_mean"), 1)
                chain(v.tensor_tensor(gd, conv, cut(bank(4), 0, NC, T), ALU.subtract))
                step(dve, v.tensor_tensor(sg, gd, gd, ALU.mult), "gn_sq")
                step(dve, v.tensor_tensor(yt[:, 2:4], ub, uc, ALU.mult), "y_b")
                dve.wait_ge(S("gn_var_done"), 1)
                step(dve, v.tensor_scalar(sg, cut(bank(5), 0, NC, T), GN_EPS, None, ALU.add), "gn_var")
                dve.wait_ge(S("u_out"), 7)
                for c in range(NC):
                    chain(v.tensor_scalar(xc[:, c], xpad[:, c, 0:T], vec[:, V_LRUW + c:V_LRUW + c + 1],
                                          vec[:, V_LRUB + c:V_LRUB + c + 1], ALU.mult, ALU.add))
                for tap in range(1, LRU_K):
                    for c in range(NC):
                        col = V_LRUW + tap * NC + c
                        step(dve, v.scalar_tensor_tensor(xc[:, c], xpad[:, c, tap:tap + T], vec[:, col:col + 1],
                                                         xc[:, c], ALU.mult, ALU.add), "lru_conv")
                for head in range(ATT_H):
                    dve.wait_ge(S("att_scores"), head + 1)
                    dve.wait_ge(S("constants_ready"), 28)
                    step(dve, v.scalar_tensor_tensor(soft[:, head, :], bank(head)[:, 0:384], HD ** -0.5,
                                                     alibi[:, head, :], ALU.mult, ALU.add), "att_biased")
                    for t, (lo, n) in enumerate(((0, P), (P, T))):
                        step(dve, v.tensor_reduce(att_m[:, 2 * head + t:2 * head + t + 1], soft[:, head, lo:lo + n], X,
                                                  ALU.max, negate=True), "att_max")
                dve.wait_ge(S("gn_std"), 1)
                chain(v.reciprocal(sg, uc))
                chain(v.tensor_tensor(gd, gd, sg, ALU.mult))
                for c in range(NC):
                    step(dve, v.tensor_scalar(gd[:, c], gd[:, c], vec[:, V_GNG + c:V_GNG + c + 1],
                                              vec[:, V_GNB + c:V_GNB + c + 1], ALU.mult, ALU.add), "gn_out")
                dve.wait_ge(S("att_exp"), 2 * ATT_H)
                chain(v.reciprocal(att_s[:], att_s[:]))
                for head in range(ATT_H):
                    for t, (lo, n) in enumerate(((0, P), (P, T))):
                        step(dve, v.tensor_scalar(soft[:, head, lo:lo + n], soft[:, head, lo:lo + n],
                                                  att_s[:, 2 * head + t:2 * head + t + 1], None, ALU.mult), "att_probs")
                dve.wait_ge(S("lru_sigmoid"), 2 * NC)
                for c in range(NC):
                    step(dve, v.tensor_scalar(r_s[:, c], r_s[:, c], lam8[:, c:c + 1], None, ALU.mult), "lru_log")
                chain(v.tensor_tensor(i_s, i_s, xc, ALU.mult))
                for head in range(ATT_H):
                    dve.wait_ge(S("att_probs_t"), head + 1)
                    step(dve, v.tensor_copy(probs_t[:, head, :], bank(head)[:, 0:384]), "att_probs_t_out")
                dve.wait_ge(S("lru_a"), 2)
                chain(v.tensor_tensor(b_s, a_s, a_s, ALU.mult))
                step(dve, v.scalar_tensor_tensor(th_s, b_s, 1.0, th_s, ALU.add, ALU.mult), "lru_sq")
                dve.wait_ge(S("lru_mult"), 1)
                chain(v.tensor_tensor(b_s, i_s, th_s, ALU.mult))
                for c in range(NC):
                    chain(v.tensor_tensor_scan(xc[:, c], a_s[:, c], b_s[:, c], 0.0, ALU.mult, ALU.add))
                dve.wait_ge(S("u_out"), 8)
                step(dve, v.tensor_tensor(yt[:, 6:8], xc, gg, ALU.mult), "y_d")
                rms("y_squares", "y_var", "y_std")
                dve.wait_ge(S("gain0_loaded"), 16)
                for t in range(NT):
                    chain(v.scalar_tensor_tensor(tmp[:, t, :], bank(2 * t, 2), stats[:, 6 + t:7 + t], gb[:, 0, :],
                                                 ALU.mult, ALU.mult))
                    step(dve, v.tensor_tensor(h[:, t, :], h[:, t, :], tmp[:, t, :], ALU.add), "x1")
                rms("x1_squares", "x1_var", "x1_std")
                for t in range(NT):
                    step(dve, v.tensor_scalar(hn[:, t, :], h[:, t, :], stats[:, 6 + t:7 + t], None, ALU.mult), "x1_normed")
                for t in range(NT):
                    dve.wait_ge(S("x1_t"), t + 1)
                    for j in range(2):
                        gain = vec[:, G_PREMLP + 4 * j:G_PREMLP + 4 * j + 4].unsqueeze(2).broadcast_to([P, 4, P])
                        step(dve, v.tensor_tensor(h2t[:, 4 * j:4 * j + 4, P * t:P * (t + 1)],
                                                  cut(bank(4 + 2 * t + j), 0, 4, P), gain, ALU.mult), "h2_t")

            @block.tensor
            def _(pe):
                m = nc.tensor
                pe.wait_ge(S("constants_ready"), 2)
                pe.wait_ge(S("x_normed"), NT)
                for t in range(NT):
                    for k in range(KD):
                        last = m.transpose(bank(2 * t + k // 4)[:, P * (k % 4):P * (k % 4 + 1)],
                                           hn[:, t, P * k:P * (k + 1)], ident[:])
                    last.then_inc(S("x_t"), 1)
                pe.wait_ge(S("vectors_loaded"), 16 * 19)
                m.transpose(bank(7)[:, 0:V_CHAN], vrows[0:V_CHAN, :], ident[0:V_CHAN, 0:V_CHAN])
                n = VECS - V_CHAN
                m.transpose(bank(7)[:, P:P + n], grows[0:n, :], ident[0:n, 0:n]).then_inc(S("vectors_t"), 1)
                pe.wait_ge(S("h_t"), 4)
                pe.wait_ge(S("vectors_ready"), 1)

                def project(pair, b):
                    chunk, at = pair // 2, (pair % 2) * 2
                    pe.wait_ge(S(f"w_in{chunk}_loaded"), 16)
                    for c in range(NC):
                        for k in range(KD):
                            last = m.matmul(bank(b)[:, T * c:T * (c + 1)], win[chunk][:, k, P * (at + c):P * (at + c + 1)],
                                            ht[:, k, :], start=(k == 0), stop=(k == KD - 1))
                    last.then_inc(S("u_done"), 1)

                for pair, b in ((0, 4), (1, 5), (2, 6), (3, 7), (4, 0), (5, 1), (6, 2)):
                    project(pair, b)
                pe.wait_ge(S("conv_done"), 1)
                pe.wait_ge(S("constants_ready"), 10)
                m.matmul(bank(4), group_mean[:], conv, start=True, stop=True).then_inc(S("gn_mean"), 1)
                for t in range(NT):
                    for k in range(KD):
                        last = m.matmul(bank(3)[:, T * t:T * (t + 1)], ht[:, k, P * t:P * (t + 1)],
                                        win[3][:, k, T:2 * T], start=(k == 0), stop=(k == KD - 1))
                last.then_inc(S("u_done"), 1)
                pe.wait_ge(S("gn_sq"), 1)
                pe.wait_ge(S("u_out"), 1)
                m.matmul(bank(5), group_mean[:], sg, start=True, stop=True).then_inc(S("gn_var_done"), 1)
                pe.wait_ge(S("u_out"), 2)
                project(8, 6)
                pe.wait_ge(S("u_out"), 6)
                pe.wait_ge(S("xs_used"), 1)
                for head in range(ATT_H):
                    r, c = HD * (head % 2), head // 2
                    for t, (lo, n) in enumerate(((0, P), (P, T))):
                        last = m.matmul(bank(head)[:, lo:lo + n], uq[r:r + HD, c, P * t:P * (t + 1)],
                                        uk[r:r + HD, c, 0:n], start=True, stop=True)
                    last.then_inc(S("att_scores"), 1)
                project(9, 7)
                pe.wait_ge(S("lru_w_loaded"), 16 * 8)
                pe.wait_ge(S("lru_conv"), (LRU_K - 1) * NC)
                pe.wait_ge(S("gn_var"), 1)
                for w in range(2):
                    for c in range(NC):
                        last = m.matmul(bank(4 + w)[:, T * c:T * (c + 1)], bd[:, w, c, :], xc[:, c, :],
                                        start=True, stop=True)
                    last.then_inc(S("lru_gates_done"), 1)
                for head in range(ATT_H):
                    pe.wait_ge(S("att_probs"), 2 * head + 2)
                    for j in range(3):
                        last = m.transpose(bank(head)[:, P * j:P * (j + 1)], soft[:, head, P * j:P * (j + 1)], ident[:])
                    last.then_inc(S("att_probs_t"), 1)
                pe.wait_ge(S("u_out"), 7)
                for head in range(ATT_H):
                    pe.wait_ge(S("att_probs_t_out"), head + 1)
                    r, c = HD * (head % 2), head // 2
                    to = bank(6)[r:r + HD, T * c:T * (c + 1)]
                    m.matmul(to[:, 0:P], uv[:, 0, HD * head:HD * (head + 1)], probs_t[:, head, 0:P], start=True, stop=True)
                    m.matmul(to[:, P:T], uv[:, 0, HD * head:HD * (head + 1)], probs_t[:, head, P:T], start=True, stop=False)
                    last = m.matmul(to[:, P:T], uv[:, 1, HD * head:HD * (head + 1)], probs_t[:, head, T:384],
                                    start=False, stop=True)
                last.then_inc(S("att_pv"), 1)
                pe.wait_ge(S("w_out_loaded"), 16)
                for k in (2, 3, 0, 1, 4, 5, 6, 7):
                    for first, signal in ((2, "y_b"), (0, "y_a"), (4, "y_c"), (6, "y_d")):
                        if k == first:
                            pe.wait_ge(S(signal), 1)
                    for t in range(NT):
                        for half in range(2):
                            last = m.matmul(bank(2 * t + half), yt[:, k, P * t:P * (t + 1)],
                                            wout[:, k, BANK * half:BANK * (half + 1)], start=(k == 2), stop=(k == 7))
                last.then_inc(S("y_done"), 1)
                pe.wait_ge(S("x1_normed"), NT)
                for t in range(NT):
                    for k in range(KD):
                        last = m.transpose(bank(4 + 2 * t + k // 4)[:, P * (k % 4):P * (k % 4 + 1)],
                                           hn[:, t, P * k:P * (k + 1)], ident[:])
                    last.then_inc(S("x1_t"), 1)

        forget({"gain0_loaded", "gain1_loaded", "meta_loaded", "w1_0_loaded", "w1_1_loaded", "w2_0_loaded", "h2_t", "dve_order"})

        with nc.Block(no_gpsimd_drain=True) as block:
            @block.sync
            def _(sp):
                w1_v = mlp_w1[0].rearrange("(k p) n -> p k n", p=P)
                w2_v = mlp_w2[0].rearrange("(f p) n -> p f n", p=P)
                sp.dma_start(w2b[1], w2_v[:, FT:2 * FT, :]).then_inc(S("w2_1_loaded"), 16)
                sp.dma_start(gb[:, 0, :], pool_scale[0].partition_broadcast(P)).then_inc(S("gain0_loaded"), 16)
                with sp.Fori(0, DFF // CHUNK // 2 - 1) as i:
                    for b in range(2):
                        sp.wait_ge(S("up_done"), i * (2 * FT) + FT * (b + 1))
                        sp.dma_start(w1b[b], w1_v[:, :, bass.ds(i * (2 * CHUNK) + CHUNK * (b + 2), CHUNK)])\
                            .then_inc(S(f"w1_{b}_loaded"), 16)
                        sp.wait_ge(S("down_done"), i * (2 * FT) + FT * (b + 2))
                        sp.dma_start(w2b[b], w2_v[:, bass.ds(i * (2 * FT) + FT * (b + 2), FT), :])\
                            .then_inc(S(f"w2_{b}_loaded"), 16)
                sp.dma_start(wq_peer, peer_wq[0].rearrange("(k p) n -> p k n", p=P)).then_inc(S("peer_wq0_loaded"), 16)

            @block.scalar
            def _(act):
                a = nc.scalar
                act.sem_inc(S("up_bank_free"), FT)
                with act.Fori(0, DFF // CHUNK // 2) as i:
                    for q in range(2 * FT):
                        act.wait_ge(S("up_done"), i * (2 * FT) + (q + 1))
                        a.activation(relu[:, q % 2, :], bank(4 + q % FT)[:, 0:T], ACT.Relu)\
                            .then_inc(S("up_bank_free"), 1)
                        act.drain()
                        act.wait_ge(S("down_done"), i * (2 * FT) + (q + 1))
                        a.activation(act2[:, q % FT, :], relu[:, q % 2, :], ACT.Square).then_inc(S("hidden_ready"), 1)
                        act.drain()
                act.wait_ge(S("mlp_done"), 1)
                for t in range(NT):
                    step(act, a.activation(sc[:, 0:D], bank(2 * t, 2), ACT.Square, accum_out=stats[:, t:t + 1]),
                         "m_squares")
                act.wait_ge(S("m_var"), 1)
                step(act, a.activation(stats[:, 6:9], stats[:, 3:6], ACT.Sqrt), "m_std")

            @block.tensor
            def _(pe):
                m = nc.tensor

                def seed(b, start):
                    return m.matmul(cut(bank(b), 0, 4, P), zeros[:], zeros[:].unsqueeze(1).broadcast_to([P, 4, P]),
                                    start=start, stop=not start)

                for b in range(4):
                    last = seed(b, True)
                last.then_inc(S("down_done"), FT)
                pe.wait_ge(S("h2_t"), 4)
                with pe.Fori(0, DFF // CHUNK // 2) as i:
                    def up(q):
                        b = q // FT
                        if q % FT == 0:
                            pe.wait_ge(S(f"w1_{b}_loaded"), i * 16 + 16)
                        pe.wait_ge(S("up_bank_free"), i * (2 * FT) + (q + 1))
                        for k in range(KD):
                            last = m.matmul(bank(4 + q % FT)[:, 0:T], w1b[b][:, k, P * (q % FT):P * (q % FT + 1)],
                                            h2t[:, k, :], start=(k == 0), stop=(k == KD - 1))
                        last.then_inc(S("up_done"), 1)

                    def down(q):
                        b = q // FT
                        if q % FT == 0:
                            pe.wait_ge(S(f"w2_{b}_loaded"), i * 16 + 16)
                        pe.wait_ge(S("hidden_ready"), i * (2 * FT) + (q + 1))
                        for t in range(NT):
                            for half in range(2):
                                last = m.matmul(bank(2 * t + half), act2[:, q % FT, P * t:P * (t + 1)],
                                                w2b[b][:, q % FT, BANK * half:BANK * (half + 1)],
                                                start=False, stop=False)
                        last.then_inc(S("down_done"), 1)

                    up(0)
                    for q in range(2 * FT):
                        if q + 1 < 2 * FT:
                            up(q + 1)
                        down(q)
                for b in range(4):
                    last = seed(b, False)
                last.then_inc(S("mlp_done"), 1)

            @block.vector
            def _(dve):
                v = nc.vector
                dve_inverse_rms(dve, X_TILES, "m")
                dve.wait_ge(S("gain1_loaded"), 16)
                for t in range(NT):
                    step(dve, v.scalar_tensor_tensor(tmp[:, t, :], bank(2 * t, 2), stats[:, 9 + t:10 + t], gb[:, 1, :],
                                                     ALU.mult, ALU.mult), "dve_order")
                    step(dve, v.tensor_tensor(h[:, t, :], h[:, t, :], tmp[:, t, :], ALU.add), "x2")
                step(dve, v.tensor_copy(iota16[:], iota16_i[:]), "dve_order")
                step(dve, v.tensor_copy(ratio[:, 0, :], ratio_i[:]), "dve_order")
                step(dve, v.reciprocal(ratio[:, 3, :], ratio[:, 0, :]), "dve_order")
                for g in range(POOL_GROUPS):
                    step(dve, v.tensor_scalar(ratio[:, g, :], ratio[:, 3, :], 2.0 ** (g + 1), 1.0, ALU.mult, ALU.max),
                         "ratio_ready")

        TILES = X_TILES + [META_TILE]
        with nc.Block(no_gpsimd_drain=True) as block:
            @block.sync
            def _(sp):
                sp.dma_start(gb[:, 1, :], norm_ffn[0].partition_broadcast(P)).then_inc(S("gain1_loaded"), 16)
                sp.dma_start(poolw, pool_w[0].rearrange("g (k p) n -> p (g k) n", p=P)).then_inc(S("pool_w_loaded"), 16)
                sp.dma_start(keys_in[0], peer_keys[0].rearrange("h w n c -> n (h w) c"))\
                    .then_inc(S("peer_keys0_loaded"), 16)

            @block.gpsimd
            def _(pool):
                for i in range(3):
                    nc.gpsimd.memset(seq[i][:, :, 0:META], 0.0).then_inc(S("pads_ready"), 1)

            @block.scalar
            def _(act):
                act.wait_ge(S("meta_loaded"), 16)
                act_squares(act, TILES, None, "pool")
                act_squares(act, TILES, "h1", "ffn0")
                peer_queries_act(act, TILES, "ffn0")

            @block.vector
            def _(dve):
                v = nc.vector
                dve_inverse_rms(dve, TILES, "pool")
                for rows, t, _ in TILES:
                    step(dve, v.tensor_scalar(normed(t)[0:rows], h[0:rows, t, :], stats[0:rows, 9 + t:10 + t], None,
                                              ALU.mult), "pool_normed")
                dve.wait_ge(S("pads_ready"), 3)
                for n, psum, k, blocks, at, cols in transposed(TILES):
                    dve.wait_ge(S("pool_t"), n + 1)
                    gain = vec[:, G_MIX0 + k:G_MIX0 + k + blocks].unsqueeze(2).broadcast_to([P, blocks, cols])
                    step(dve, v.tensor_tensor(seq[0][:, k:k + blocks, META + at:META + at + cols], psum, gain,
                                              ALU.mult), "pool_t_out")
                sums = [seq[0], seq[1], seq[2], seq[1], seq[2]]
                for g in range(POOL_GROUPS):
                    src, to, w, k = sums[g], sums[g + 1], 2 ** g, 2 * g
                    step(dve, v.tensor_tensor(to[:, k:KD, META:PADL], src[:, k:KD, META:PADL],
                                              src[:, k:KD, META - w:PADL - w], ALU.add), "dve_order")
                    r = ratio[:, g, :].unsqueeze(1).broadcast_to([P, 2, META])
                    part = work[:, 0, 0:2 * META].rearrange("p (a n) -> p a n", a=2)
                    body = to[:, k:k + 2, :]
                    step(dve, v.tensor_tensor(part, body[:, :, META:2 * META], r, ALU.mult), "dve_order")
                    for lo, n, s in ((0, META, part), (META, T, body[:, :, 2 * META:])):
                        step(dve, v.scalar_tensor_tensor(pooled[:, k:k + 2, lo:lo + n], s, 0.5 ** (g + 1),
                                                         seq[0][:, k:k + 2, META + lo:META + lo + n],
                                                         ALU.mult, ALU.subtract), "pooled")
                for n, (rows, t, _) in enumerate(TILES):
                    dve.wait_ge(S("mixed"), n + 1)
                    dve.wait_ge(S("gain0_loaded"), 32)
                    to = tmp_m if t == NT else tmp[:, t, :]
                    step(dve, v.tensor_tensor(to, tile_banks(t), gb[0:rows, 0, :], ALU.mult), "dve_order")
                    step(dve, v.tensor_tensor(h[0:rows, t, :], h[0:rows, t, :], to, ALU.add), "h1")
                peer_norm_dve(dve, TILES, "ffn0", gb[:, 1, :], "gain1_loaded")
                peer_scores_dve(dve, 0, "ffn0")
                dve.wait_ge(S("rep_t"), 1)
                step(dve, v.tensor_copy(rept[:], bank(5)[:, 0:META]), "rept_ready")

            @block.tensor
            def _(pe):
                m = nc.tensor
                pe_transposes(pe, TILES, "pool")
                pe.wait_ge(S("pool_t_out"), 5)
                pe.wait_ge(S("pool_w_loaded"), 16)
                pe.wait_ge(S("pooled"), 2 * POOL_GROUPS)
                for n, (rows, t, at) in enumerate(TILES):
                    for g in range(POOL_GROUPS):
                        for k in range(2):
                            last = m.matmul(tile_banks(t)[:, GW * g:GW * (g + 1)], pooled[:, 2 * g + k, at:at + rows],
                                            poolw[:, 2 * g + k, :], start=(k == 0), stop=(k == 1))
                    last.then_inc(S("mixed"), 1)
                pe_transposes(pe, TILES, "ffn0")
                peer_scores_pe(pe, TILES, 0, "ffn0")
                m.transpose(bank(5)[:, 0:META], rep[:, :, :].rearrange("p h t -> p (h t)"), ident[0:META, 0:META])\
                    .then_inc(S("rep_t"), 1)

        with nc.Block() as block:
            @block.sync
            def _(sp):
                sp.dma_start(wkv, w_kv.rearrange("(k p) n -> p k n", p=P)).then_inc(S("w_kv_loaded"), 16)
                sp.dma_start(gb[:, 0, :], norm_ffn[1].partition_broadcast(P)).then_inc(S("gain0_loaded"), 16)

            @block.gpsimd
            def _(pool):
                peer_gpsimd(pool, 0)

            @block.scalar
            def _(act):
                peer_scalar(act, 0)

            @block.vector
            def _(dve):
                peer_vector(dve, 0)

            @block.tensor
            def _(pe):
                peer_tensor(pe, 0)

        with nc.Block(no_gpsimd_drain=True) as block:
            def kq(n):
                return (kv_in, wkv, k_t, L) if n < KD else (q_in, wq_att, q_t, T)

            squares = [work[:, 0:3, :].rearrange("p a n -> p (a n)")[:, L * i:L * (i + 1)] for i in range(2)]
            k_root = [diag[:, :, :].rearrange("p a n -> p (a n)")[:, 0:L], ua[:, KD * (L + T):KD * (L + T) + L]]

            @block.sync
            def _(sp):
                sp.dma_start(wq_att, w_q[0].rearrange("(k p) n -> p k n", p=P)).then_inc(S("w_q_loaded"), 16)
                sp.dma_start(wo_att, w_o[0].rearrange("(k p) n -> p k n", p=P)).then_inc(S("w_o_loaded"), 16)
                sp.wait_ge(S("v_done"), 6)
                sp.dma_start(wq_peer, peer_wq[1].rearrange("(k p) n -> p k n", p=P)).then_inc(S("peer_wq1_loaded"), 16)
                sp.wait_ge(S("kq_done"), 2 * KD)
                sp.dma_start(keys_in[1], peer_keys[1].rearrange("h w n c -> n (h w) c"))\
                    .then_inc(S("peer_keys1_loaded"), 16)

            @block.gpsimd
            def _(pool):
                g = nc.gpsimd
                step(pool, g.memset(eps_col[:], EPS), "masks_ready")
                pool.wait_ge(S("kq_out"), 2 * KD)
                step(pool, g.memset(neg_mask, 0.0), "masks_ready")
                for at in (META, Z - P):
                    step(pool, g.affine_select(out=neg_mask[:, at:at + P], in_=neg_mask[:, at:at + P],
                                               compare_op=ALU.is_gt, fill=NEG, base=0, pattern=[[-1, P]],
                                               channel_multiplier=1), "masks_ready")
                step(pool, g.memset(seg, 1.0), "masks_ready")
                step(pool, g.memset(seg[:, META + P - 1:META + P], 0.0), "masks_ready")
                pool.wait_ge(S("v_out"), 6)
                with pool.Fori(0, KD // 2) as ii:
                    for par in range(2):
                        i = ii * 2 + par
                        pool.wait_ge(S("pv_done"), i * 2 + 2)
                        passed(pool)
                        g.tensor_copy(k_now[:, par:par + 1, :], k_t[:, bass.ds(i, 1), :])
                        g.tensor_copy(q_now[:, par:par + 1, :], q_t[:, bass.ds(i, 1), :])
                        g.tensor_copy(v_now[0:META, par, 2, :], v_meta[:, bass.ds(i * P, P)])
                        g.tensor_copy(v_now[:, par, 0:NT, :], hn[:, :, bass.ds(i * P, P)]).then_inc(S("staged"), 1)

            @block.scalar
            def _(act):
                a = nc.scalar
                act_squares(act, TILES, None, "kv")
                act.wait_ge(S("masks_ready"), 1)

                def square(n):
                    act.wait_ge(S("kq_done"), n + 1)
                    w = kq(n)[3]
                    step(act, a.activation(squares[n % 2][:, 0:w], bank(5 + n % 3)[:, 0:w], ACT.Square), "kq_squares")

                def root(n):
                    act.wait_ge(S("kq_means"), n + 1)
                    if n >= 2:
                        act.wait_ge(S("kq_out"), n - 1)
                    w = kq(n)[3]
                    step(act, a.activation(k_root[n % 2][:, 0:w], bank(n % 2)[:, 0:w], ACT.Sqrt, bias=eps_col[:]),
                         "kq_roots")

                def v_copies():
                    for j in range(6):
                        t, half = j // 2, j % 2
                        act.wait_ge(S("v_done"), j + 1)
                        rows = META if t == NT else P
                        to = v_meta if t == NT else hn[:, t, :]
                        step(act, a.activation(to[:, BANK * half:BANK * (half + 1)], bank(2 + j % 3)[0:rows], ACT.Copy),
                             "v_out")

                square(0)
                for n in range(1, 2 * KD + 1):
                    if n == KD:
                        square(n)
                        root(n - 1)
                        v_copies()
                        continue
                    if n < 2 * KD:
                        square(n)
                    root(n - 1)

                act.sem_inc(S("wt_meta_out"), 2)
                act.sem_inc(S("att_y_out"), 2)

                def softplus_part(n, q):
                    act.wait_ge(S("z_masked"), n + 1)
                    l = ls[:, q, :]
                    a.activation(l, zs[:, q, :], ACT.Abs)
                    act.drain()
                    a.activation(l, l, ACT.Exp, scale=-1.0)
                    act.drain()
                    a.activation(l, l, ACT.Ln, bias=1.0).then_inc(S("log_done"), 1)

                def weights(n, q):
                    act.wait_ge(S("log_w"), n + 1)
                    a.activation(ws[:, q, :], zs[:, q, :], ACT.Exp).then_inc(S("w_ready"), 1)

                def meta_weights_out(n, q):
                    act.wait_ge(S("wt_done"), n + 1)
                    act.wait_ge(S("pv_done"), n + 3)
                    a.activation(wt_meta[0:META, q % 2, :], bank(4 + q % 2)[0:META, 0:T], ACT.Copy)\
                        .then_inc(S("wt_meta_out"), 1)

                def y_out(i, par):
                    act.wait_ge(S("pv_done"), i * 2 + 6)
                    passed(act)
                    a.activation(att_y[:, bass.ds(i, 1), :], cut(bank(6 + par), 0, 1, T), ACT.Copy)\
                        .then_inc(S("att_y_out"), 1)

                def four_heads(ii, first=False, last=False):
                    for q in range(4):
                        n = ii * 4 + q
                        if not (last and q == 3):
                            softplus_part(n + 1, (q + 1) % 4)
                        weights(n, q)
                        if not (first and q == 0):
                            meta_weights_out(n - 1, (q - 1) % 4)
                        if q % 2 and not (first and q == 1):
                            y_out(ii * 2 + (q // 2 - 1), (q // 2 + 1) % 2)
                    if last:
                        meta_weights_out(n, q)
                        y_out(ii * 2 + 1, 1)

                softplus_part(0, 0)
                four_heads(0, first=True)
                with act.Fori(1, SB_H // 4 - 1) as ii:
                    four_heads(ii)
                four_heads(SB_H // 4 - 1, last=True)
                act_squares(act, X_TILES, "h3", "ffn1")
                peer_queries_act(act, X_TILES, "ffn1")

            @block.vector
            def _(dve):
                v = nc.vector
                dve_inverse_rms(dve, TILES, "kv")
                for rows, t, _ in TILES:
                    step(dve, v.tensor_scalar(normed(t, "kv")[0:rows], h[0:rows, t, :], stats[0:rows, 9 + t:10 + t],
                                              None, ALU.mult), "kv_normed")
                for n, psum, k, blocks, at, cols in transposed(TILES):
                    dve.wait_ge(S("kv_t"), n + 1)
                    uses = [(kv_in, G_KV, at)] + ([(q_in, G_MIX1, at - META)] if cols == P else [])
                    for to, gains, col in uses:
                        gain = vec[:, gains + k:gains + k + blocks].unsqueeze(2).broadcast_to([P, blocks, cols])
                        step(dve, v.tensor_tensor(to[:, k:k + blocks, col:col + cols], psum, gain, ALU.mult), "kv_t_out")
                step(dve, v.tensor_scalar(vec[:, V_Q:V_Q + 1], vec[:, V_Q:V_Q + 1], HD ** -0.5, None, ALU.mult),
                     "dve_order")
                for n in range(2 * KD):
                    _, _, to, w = kq(n)
                    dve.wait_ge(S("kq_roots"), n + 1)
                    r = k_root[n % 2][:, 0:w]
                    col = V_K if n < KD else V_Q
                    step(dve, v.reciprocal(r, r), "dve_order")
                    step(dve, v.scalar_tensor_tensor(to[:, n % KD, :], bank(5 + n % 3)[:, 0:w], vec[:, col:col + 1], r,
                                                     ALU.mult, ALU.mult), "kq_out")
                dve.wait_ge(S("masks_ready"), 6)
                dve.sem_inc(S("wt_out"), 2)

                def mask(n, q):
                    dve.wait_ge(S("z_done"), n + 1)
                    v.tensor_tensor(zs[:, q, :], bank(q % 2)[:, 0:Z], neg_mask, ALU.add).then_inc(S("z_masked"), 1)

                def log_weights(n, q):
                    z, l, s = zs[:, q, :], ls[:, q, :], ws[:, q, :]
                    dve.wait_ge(S("log_done"), n + 1)
                    v.scalar_tensor_tensor(l, z, 0.0, l, ALU.max, ALU.add)
                    dve.drain()
                    v.tensor_tensor_scan(s[:, ::-1], seg[:, ::-1], l[:, ::-1], 0.0, ALU.mult, ALU.add)
                    dve.drain()
                    v.tensor_tensor(z, z, s, ALU.subtract).then_inc(S("log_w"), 1)

                def weights_out(n, q):
                    dve.wait_ge(S("wt_done"), n + 1)
                    dve.wait_ge(S("pv_done"), n + 3)
                    v.tensor_copy(wt[:, q % 2, :], bank(2 + q % 2)[:, 0:3 * P]).then_inc(S("wt_out"), 1)

                def four_heads(ii, first=False, last=False):
                    for q in range(4):
                        n = ii * 4 + q
                        if not (last and q == 3):
                            mask(n + 1, (q + 1) % 4)
                        log_weights(n, q)
                        if not (first and q == 0):
                            weights_out(n - 1, (q - 1) % 4)
                    if last:
                        weights_out(n, q)

                mask(0, 0)
                four_heads(0, first=True)
                with dve.Fori(1, SB_H // 4 - 1) as ii:
                    four_heads(ii)
                four_heads(SB_H // 4 - 1, last=True)
                for t in range(NT):
                    dve.wait_ge(S("att_projected"), t + 1)
                    step(dve, v.tensor_tensor(h[:, t, :], h[:, t, :], bank(2 * t, 2), ALU.add), "h3")
                peer_norm_dve(dve, X_TILES, "ffn1", gb[:, 0, :], "gain0_loaded")
                peer_scores_dve(dve, 1, "ffn1")

            @block.tensor
            def _(pe):
                m = nc.tensor
                pe_transposes(pe, TILES, "kv")
                pe.wait_ge(S("kv_t_out"), 9)

                def project(n):
                    src, w, _, width = kq(n)
                    if n >= 3:
                        pe.wait_ge(S("kq_out"), n - 2)
                    for k in range(KD):
                        last = m.matmul(bank(5 + n % 3)[:, 0:width], w[:, k, P * (n % KD):P * (n % KD + 1)], src[:, k, :],
                                        start=(k == 0), stop=(k == KD - 1))
                    last.then_inc(S("kq_done"), 1)

                def mean(n):
                    width = kq(n)[3]
                    if n >= 2:
                        pe.wait_ge(S("kq_roots"), n - 1)
                    pe.wait_ge(S("kq_squares"), n + 1)
                    m.matmul(bank(n % 2)[:, 0:width], group_mean[:], squares[n % 2][:, 0:width], start=True, stop=True)\
                        .then_inc(S("kq_means"), 1)

                pe.wait_ge(S("w_kv_loaded"), 16)
                project(0)
                for n in range(1, KD):
                    project(n)
                    mean(n - 1)
                mean(KD - 1)
                pe.wait_ge(S("w_q_loaded"), 16)
                project(KD)
                for j in range(6):
                    rows, t, at = TILES[j // 2]
                    half = j % 2
                    if j >= 3:
                        pe.wait_ge(S("v_out"), j - 2)
                    for k in range(KD):
                        last = m.matmul(bank(2 + j % 3)[0:rows], kv_in[:, k, at:at + rows],
                                        wkv[:, k, D + BANK * half:D + BANK * (half + 1)],
                                        start=(k == 0), stop=(k == KD - 1))
                    last.then_inc(S("v_done"), 1)
                for n in range(KD + 1, 2 * KD):
                    project(n)
                    mean(n - 1)
                mean(2 * KD - 1)

                pe.wait_ge(S("kq_roots"), 2 * KD)
                pe.wait_ge(S("kq_out"), 2 * KD)
                pe.sem_inc(S("pv_done"), 4)

                def z(n, q, i):
                    s, par = q % 2, (q // 2) % 2
                    if s == 0:
                        pe.wait_ge(S("staged"), i + 1)
                    if not (isinstance(n, int) and n < 2):
                        pe.wait_ge(S("z_masked"), n - 1)
                    r = HD * s
                    for t, (lo, keys) in enumerate(((0, META + P), (META + P, L))):
                        last = m.matmul(bank(s)[:, lo:lo + keys], q_now[r:r + HD, par, P * t:P * (t + 1)],
                                        k_now[r:r + HD, par, 0:keys], start=True, stop=True)
                    last.then_inc(S("z_done"), 1)

                def transpose_weights(n, q):
                    pe.wait_ge(S("wt_out"), n + 1)
                    pe.wait_ge(S("wt_meta_out"), n + 1)
                    pe.wait_ge(S("w_ready"), n + 1)
                    w = ws[:, q, :]
                    m.transpose(bank(4 + q % 2)[0:META, 0:P], w[:, 0:META], ident[:])
                    m.transpose(bank(4 + q % 2)[0:META, P:T], w[:, META + P:2 * META + P], ident[:])
                    for to, at in ((0, META), (P, 2 * META + P), (2 * P, 2 * META + 2 * P)):
                        last = m.transpose(bank(2 + q % 2)[:, to:to + P], w[:, at:at + P], ident[:])
                    last.then_inc(S("wt_done"), 1)

                def pv(n, q, i):
                    s, par = q % 2, (q // 2) % 2
                    if s == 0:
                        pe.wait_ge(S("att_y_out"), i + 1)
                    pe.wait_ge(S("wt_out"), n + 3)
                    pe.wait_ge(S("wt_meta_out"), n + 3)
                    r = HD * s
                    y = bank(6 + par)[r:r + HD, 0:T]
                    v0, v1, vm = v_now[:, par, 0, r:r + HD], v_now[:, par, 1, r:r + HD], v_now[0:META, par, 2, r:r + HD]
                    m.matmul(y[:, 0:P], v0, wt[:, s, 0:P], start=True, stop=False)
                    m.matmul(y[:, 0:P], vm, wt_meta[0:META, s, 0:P], start=False, stop=True)
                    m.matmul(y[:, P:T], v0, wt[:, s, P:T], start=True, stop=False)
                    m.matmul(y[:, P:T], v1, wt[:, s, T:3 * P], start=False, stop=False)
                    m.matmul(y[:, P:T], vm, wt_meta[0:META, s, P:T], start=False, stop=True).then_inc(S("pv_done"), 1)

                def four_heads(ii, first=False, last=False):
                    for q in range(4):
                        n, i = ii * 4 + q, ii * 2 + q // 2
                        if not (last and q == 3):
                            z(n + 1, q + 1, ii * 2 + (q + 1) // 2)
                        transpose_weights(n, q)
                        if not (first and q == 0):
                            pv(n - 1, (q - 1) % 4, ii * 2 + (q - 1) // 2)
                    if last:
                        pv(n, q, i)

                z(0, 0, 0)
                four_heads(0, first=True)
                with pe.Fori(1, SB_H // 4 - 1) as ii:
                    four_heads(ii)
                four_heads(SB_H // 4 - 1, last=True)
                pe.wait_ge(S("w_o_loaded"), 16)
                pe.wait_ge(S("att_y_out"), KD + 2)
                for t in range(NT):
                    for half in range(2):
                        for k in range(KD):
                            last = m.matmul(bank(2 * t + half), att_y[:, k, P * t:P * (t + 1)],
                                            wo_att[:, k, BANK * half:BANK * (half + 1)],
                                            start=(k == 0), stop=(k == KD - 1))
                    last.then_inc(S("att_projected"), 1)
                pe_transposes(pe, X_TILES, "ffn1")
                peer_scores_pe(pe, X_TILES, 1, "ffn1")

        with nc.Block() as block:
            @block.sync
            def _(sp):
                out_v = out[0].rearrange("(t p) d -> p t d", p=P)
                for t in range(NT):
                    sp.wait_ge(S("tile_out1"), t + 2)
                    sp.dma_start(out_v[:, t, :], h[:, t, :]).then_inc(S("out_stored"), 16)
                sp.wait_ge(S("out_stored"), 16 * NT)

            @block.gpsimd
            def _(pool):
                peer_gpsimd(pool, 1)

            @block.scalar
            def _(act):
                peer_scalar(act, 1)

            @block.vector
            def _(dve):
                peer_vector(dve, 1)

            @block.tensor
            def _(pe):
                peer_tensor(pe, 1)


_INS = ["x", "pre_mix_g", "w_in", "conf_dw_w", "conf_dw_b", "conf_gn_g", "conf_gn_b", "sconv_w", "lru_conv_w",
        "lru_conv_b", "lru_wa", "lru_ba", "lru_wx", "lru_bx", "lru_lam", "w_out", "post_mix_g", "pre_mlp_g", "mlp_w1",
        "mlp_w2", "post_mlp_g", "meta_tokens_2", "norm_mix_2", "norm_ffn_2", "pool_w_2", "pool_scale_2", "kv_norm_2",
        "w_kv_2", "k_norm_2", "w_q_2", "q_norm_2", "w_o_2", "peer_wq_2", "peer_keys_2", "peer_u_2", "peer_v_2"]


def kernel(**inputs):
    import numpy as np
    import concourse.bacc as bacc
    from concourse.bass_utils import run_bass_kernel_spmd

    nc = bacc.Bacc("TRN2", target_bir_lowering=False, num_devices=1)
    arrays, args = {}, []
    for name in _INS:
        a = np.ascontiguousarray(inputs[name])
        arrays[f"in_{name}"] = a
        args.append(nc.dram_tensor(f"in_{name}", a.shape, mybir.dt.from_np(a.dtype), kind="ExternalInput").ap())
    args.append(nc.dram_tensor("out", (1, T, D), F32, kind="ExternalOutput").ap())
    program(nc, *args)
    return run_bass_kernel_spmd(nc, [arrays], core_ids=[0]).results[0]["out"]
```

```python
import math
from contextlib import ExitStack

import concourse.bass as bass
from concourse import mybir

F32, BF16 = mybir.dt.float32, mybir.dt.bfloat16
I32, U32 = mybir.dt.int32, mybir.dt.uint32
ALU = mybir.AluOpType
ACT = mybir.ActivationFunctionType
X = mybir.AxisListType.X

P = 128
BANK = 512
D = 1024
KD = D // P
T = 256
NT = T // P
META = 16
L = META + T
GW = 256
NC = GW // P
DFF = 4096
CHUNK = 512
FT = CHUNK // P
CONF_K, SC_K, LRU_K = 31, 3, 4
ATT_H, HD = 4, 64
LRU_C = 8.0
EPS, GN_EPS = 1e-6, 1e-5
PH, KEYS, TOPK = 8, 128, 16
EXPERTS = KEYS * KEYS
RING = 8
DIAGS = 4
NEG = -1.0e30
MASKED = -3.0e38
POOL_GROUPS = 4

V_CONF = 0
V_SC = V_CONF + CONF_K * NC
V_LRUW = V_SC + SC_K * NC
V_DWB = V_LRUW + LRU_K * NC
V_GNG, V_GNB, V_LRUB, V_BA, V_BX, V_LAM = (V_DWB + NC * i for i in range(1, 7))
V_CHAN = V_LAM + NC
G_PREMIX, G_PREMLP, G_MIX0, G_KV, G_MIX1 = (V_CHAN + KD * i for i in range(5))
V_GAIN = 5 * KD
V_K = V_CHAN + V_GAIN
V_Q = V_K + 1
VECS = V_Q + 1


def program(nc, x, pre_mix_g, w_in, conf_dw_w, conf_dw_b, conf_gn_g, conf_gn_b, sconv_w, lru_conv_w,
            lru_conv_b, lru_wa, lru_ba, lru_wx, lru_bx, lru_lam, w_out, post_mix_g, pre_mlp_g, mlp_w1,
            mlp_w2, post_mlp_g, meta_tokens, norm_mix, norm_ffn, pool_w, pool_scale, kv_norm, w_kv,
            k_norm, w_q, q_norm, w_o, peer_wq, peer_keys, peer_u, peer_v, out):
    ctx = ExitStack()
    with ctx:
        def sb(name, shape, dt=F32):
            return ctx.enter_context(nc.sbuf_tensor(name, shape, dt))

        named, count = {}, {}

        def S(name):
            if name not in named:
                named[name] = nc.alloc_semaphore(name=name)
                count[name] = 0
            return named[name]

        def forget(kept):
            gone = [name for name in named if name not in kept]
            nc.clear_and_free_semaphores([named.pop(name) for name in gone])
            for name in gone:
                del count[name]
            nc.all_engine_barrier()

        def step(engine, instruction, signals):
            instruction.then_inc(S(signals), 1)
            count[signals] += 1
            engine.wait_ge(S(signals), count[signals])

        big = sb("big", [P, 2 * 16384])
        h = sb("residual", [P, 3, D])
        hn = sb("normed", [P, NT, D])
        ua = sb("ua", [P, 18 * 256])
        sc = sb("sc", [P, 17 * 256])
        gb = sb("gain_rows", [P, 2, D])
        vec = sb("vectors", [P, VECS])
        ident = sb("ident", [P, P])
        group_mean = sb("group_mean", [P, P])
        zeros = sb("zeros", [P, P], BF16)
        rep = sb("rep", [META, PH, META])
        eps_col = sb("eps", [P, 1])
        rept = sb("rept", [P, META])
        stats = sb("stats", [P, 12])
        lam_s = sb("softplus_lam", [P, 6 * NC])
        lam8 = sb("minus_8_softplus", [P, NC])
        att_m = sb("att_m", [P, 2 * ATT_H])
        att_s = sb("att_s", [P, 2 * ATT_H])
        diag = sb("diag", [P, DIAGS, P])
        ratio = sb("ratio", [P, POOL_GROUPS, META])
        ratio_i = sb("ratio_i", [P, META], I32)
        work = sb("work", [P, 3, 256])
        ints = sb("ints", [P, 2, TOPK], I32)
        half_v = sb("half_v", [P, 2, TOPK])
        half_i = sb("half_i", [P, 2, TOPK], U32)
        half_f = sb("half_f", [P, 2, TOPK])
        best = sb("best", [P, 2, TOPK])
        best_at = sb("best_at", [P, TOPK], U32)
        pos_f = sb("pos_f", [P, 2, TOPK])
        picked = sb("picked", [P, 2, TOPK])
        expert = sb("expert", [P, 2, TOPK], U32)
        neg_best = sb("neg_best", [P, 2])
        gate = sb("gate", [P, 2, TOPK])
        gate_sum = sb("gate_sum", [P, 2])
        dots = sb("dots", [P, 2, TOPK])
        weight = sb("weight", [P, 2, TOPK])
        iota16 = sb("iota16", [P, TOPK])
        iota16_i = sb("iota16_i", [P, TOPK], I32)
        ps = ctx.enter_context(nc.psum_tensor("ps", [P, 8 * BANK], F32))

        def bank(b, n=1):
            return ps[:, BANK * b:BANK * (b + n)]

        def cut(ap, lo, a, b):
            return ap[:, lo:lo + a * b].rearrange("p (a b) -> p a b", a=a)

        win = [cut(big, 4096 * c, KD, CHUNK) for c in range(5)]
        wout = cut(big, 5 * 4096, KD, D)
        tail = 28672
        alibi = cut(big, tail, ATT_H, 384)
        soft = cut(big, tail + 1536, ATT_H, 384)
        bd = big[:, tail + 3072:tail + 3584].rearrange("p (w c n) -> p w c n", w=2, c=NC)
        alibi_i = big[:, tail + 3584:tail + 3968].bitcast(I32)
        probs_t = cut(big, 0, ATT_H, 384)
        r_s, i_s, a_s, th_s, b_s = (cut(big, 1536 + 512 * i, NC, T) for i in range(5))
        sg, ub, uc, uq, uk, uv, gg, xc, gd = (cut(ua, 512 * i, NC, T) for i in range(9))
        zpad = cut(sc, 0, NC, CONF_K - 1 + T)
        spad = cut(sc, 572, NC, SC_K - 1 + T)
        xpad = cut(sc, 1088, NC, LRU_K - 1 + T)
        conv = cut(sc, 1606, NC, T)
        ht = cut(sc, 2118, KD, T)
        yt = hn[:, :, :].rearrange("p t (a n) -> p (t a) n", n=T)
        tmp_m = sc[0:META, 2048:3072]
        tmp = sc[:, 0:2048].rearrange("p (t n) -> p t n", t=NT)
        lam = [lam_s[:, NC * i:NC * (i + 1)] for i in range(6)]
        vrows = gb[:, 1, 0:P]
        grows = gb[:, 1, P:2 * P]
        w1b = [cut(big, 4096, KD, CHUNK), cut(big, 8192, KD, CHUNK)]
        w2b = [cut(big, 12288, FT, D), cut(big, 0, FT, D)]
        h2t = cut(ua, 0, KD, T)
        relu = cut(sc, 0, 2, T)
        act2 = cut(sc, 512, 4, T)
        KV0 = META + P
        PADL = META + L
        keys_in = [cut(big, 12672, 2 * PH, KEYS), cut(sc, 2048, 2 * PH, KEYS)]
        keys_t = gb[:, :, :].rearrange("p a (j n) -> p (a j) n", n=KEYS)
        q_meta = big[:, KD * KV0:KD * KV0 + 2048].rearrange("p (w h n) -> p w h n", w=2, h=PH)
        seq = [cut(big, PADL * KD * i, KD, PADL) for i in range(3)]
        hnt = cut(big, 0, KD, KV0)
        pooled = cut(big, 7168, KD, L)
        hnm = big[0:META, 9600:9600 + D]
        poolw = cut(big, 10624, 2 * POOL_GROUPS, GW)
        qt = cut(ua, 0, 2 * PH, KV0)
        hnt_x1, q_rows, q_cols = cut(ua, 3328, KD, P), ua[:, 2304:2560], cut(ua, 2560, 2, P)
        scores = cut(sc, 0, 2 * PH + 1, 256)
        W = 16384
        wq_peer = cut(big, W, KD, 2 * D)
        wkv = cut(big, W, KD, 2 * D)
        wq_att = cut(big, 0, KD, D)
        wo_att = cut(big, 8192, KD, D)
        q_in, kv_in1 = cut(sc, 0, KD, T), cut(sc, KD * T, KD, P)
        kv_in0 = cut(ua, KD * L, KD, KV0)
        k_t, q_t = cut(ua, 0, KD, L), cut(ua, KD * L, KD, T)
        v_meta = gb[0:META, 1, :]
        Z = META + P + L
        zs, ls, ws = (cut(big, 4 * Z * i, 4, Z) for i in range(3))
        wt = cut(big, 12 * Z, 2, 3 * P)
        wt_meta = cut(big, 12 * Z + 768, 2, T)
        k_now = cut(big, 12 * Z + 1280, 2, L)
        q_now = cut(big, 12 * Z + 1824, 2, T)
        v_now = big[:, 12 * Z + 2336:12 * Z + 3104].rearrange("p (a t n) -> p a t n", a=2, t=3)
        neg_mask = diag[:, :, :].rearrange("p a n -> p (a n)")[:, 0:Z]
        seg = work[:, :, :].rearrange("p a n -> p (a n)")[:, 0:Z]
        att_y = cut(sc, 0, KD, T)
        ring_u = [big[:, RING * D + D * i:RING * D + D * (i + 1)] for i in range(RING)]
        ring_v = [big[:, D * i:D * (i + 1)] for i in reversed(range(RING))]
        V_EARLY = 4

        X_TILES = [(P, t, META + P * t) for t in range(NT)]
        META_TILE = (META, NT, 0)

        def normed(t, tag="ffn0"):
            return (v_meta if tag == "kv0" else hnm) if t == NT else hn[:, t, :]

        def tile_banks(t):
            return bank(4, 2)[0:META] if t == NT else bank(2 * t, 2)

        def passed(engine):
            engine.sem_inc(S("waits_passed"), 1)

        def act_squares(act, tiles, after, tag):
            for n, (rows, t, _) in enumerate(tiles):
                if after:
                    act.wait_ge(S(after), 2 if after == "tile_out0" else n + 1)
                scratch = ua[0:rows, KD * L:KD * L + D] if tag[:2] == "kv" else ua[0:rows, 0:D]
                step(act, nc.scalar.activation(scratch, h[0:rows, t, :], ACT.Square,
                                               accum_out=stats[0:rows, t:t + 1]), tag + "_squares")
                act_root_mean(act, rows, t, tag)

        def act_root_mean(act, rows, t, tag):
            step(act, nc.scalar.activation(stats[0:rows, 6 + t:7 + t], stats[0:rows, t:t + 1], ACT.Sqrt, scale=1.0 / D,
                                           bias=eps_col[0:rows]), tag + "_std")

        def dve_inverse_rms(dve, n, rows, t, tag):
            dve.wait_ge(S(tag + "_std"), n + 1)
            step(dve, nc.vector.reciprocal(stats[0:rows, 9 + t:10 + t], stats[0:rows, 6 + t:7 + t]), tag + "_inverse")

        def transposed_bank(t, tag):
            return {0: 4, NT: 6}[t] if tag == "kv0" else 2 * t

        def pe_transposes(pe, tiles, tag, before=0):
            for n, (rows, t, _) in enumerate(tiles, before):
                pe.wait_ge(S(tag + "_normed"), n + 1)
                for k in range(KD):
                    b = transposed_bank(t, tag)
                    to = bank(b)[:, META * k:META * (k + 1)] if t == NT else \
                        bank(b + k // 4)[:, P * (k % 4):P * (k % 4 + 1)]
                    last = nc.tensor.transpose(to, normed(t, tag)[0:rows, P * k:P * (k + 1)], ident[0:rows, 0:rows])
                last.then_inc(S(tag + "_t"), 1)

        def transposed(tiles, tag="ffn"):
            for n, (rows, t, at) in enumerate(tiles):
                b = transposed_bank(t, tag)
                if t == NT:
                    yield n, cut(bank(b), 0, KD, META), 0, KD, at, META
                else:
                    for j in range(2):
                        yield n, cut(bank(b + j), 0, 4, P), 4 * j, 4, at, P

        def peer_norm_dve(dve, layer, tag, gains, gains_loaded, last_rows):
            v = nc.vector
            tiles = peer_tiles(layer)

            def norm(n, rows, t):
                dve_inverse_rms(dve, n, rows, t, tag)
                step(dve, v.scalar_tensor_tensor(normed(t)[0:rows], h[0:rows, t, :], stats[0:rows, 9 + t:10 + t],
                                                 gains[0:rows], ALU.mult, ALU.mult), tag + "_normed")

            dve.wait_ge(S(gains_loaded), 16 * (2 if gains_loaded == "gain1_loaded" else 3))
            for n, (rows, t, _) in enumerate(tiles):
                norm(n, rows, t)
            last_rows()
            for n, psum, k, blocks, at, cols in transposed(tiles):
                dve.wait_ge(S(tag + "_t"), n + 1)
                step(dve, v.tensor_copy(hnt[:, k:k + blocks, at:at + cols], psum), tag + "_t_out")
            norm(len(tiles), P, 1)
            peer_keys_dve(dve, layer, tag)
            for _, psum, k, blocks, _, _ in transposed(X_TILES[1:]):
                dve.wait_ge(S(tag + "_t"), len(tiles) + 1)
                step(dve, v.tensor_copy(hnt_x1[:, k:k + blocks, :], psum), tag + "_t1_out")

        def peer_tiles(layer):
            return [X_TILES[0]] + ([META_TILE] if layer == 0 else [])

        META_UNIT = PH

        def unit_of(layer, tile, head):
            return tile * (PH + 1 - layer) + head

        def peer_scores_pe(pe, layer, tag):
            m = nc.tensor
            tiles = peer_tiles(layer)
            c0 = META * layer
            pe_transposes(pe, tiles, tag)
            pe.wait_ge(S(tag + "_t_out"), sum(1 for _ in transposed(tiles)))
            if layer == 0:
                for half in range(2):
                    m.matmul(bank(6 + half), rep[:, :, :].rearrange("p h t -> p (h t)"),
                             hnm[:, BANK * half:BANK * (half + 1)], start=True, stop=True).then_inc(S("meta_rows"), 1)
                m.transpose(bank(5)[:, 0:META], rep[:, :, :].rearrange("p h t -> p (h t)"), ident[0:META, 0:META])\
                    .then_inc(S("rep_t"), 1)
            pe.wait_ge(S(f"peer_keys{layer}_loaded"), 16)
            for j in range(2 * PH):
                last = m.transpose(bank(j // 4)[:, P * (j % 4):P * (j % 4 + 1)], keys_in[layer][:, j, :], ident[:])
                if j % 4 == 3:
                    last.then_inc(S(tag + "_keys_t"), 1)

            def queries(hp):
                if hp >= 2:
                    pe.wait_ge(S(tag + "_q_out"), hp - 1)
                for k in range(KD):
                    last = m.matmul(bank(4 + hp % 2)[:, 0:KV0 - c0], wq_peer[:, k, P * hp:P * (hp + 1)],
                                    hnt[:, k, c0:KV0], start=(k == 0), stop=(k == KD - 1))
                last.then_inc(S(tag + "_q_done"), 1)

            def scores_of(head):
                pe.wait_ge(S(tag + "_q_out"), 2 * head + 2)
                if head >= 2:
                    pe.wait_ge(S(tag + "_scores_out"), head - 1)
                for p in range(2):
                    last = m.matmul(bank(head % 2)[:, P * p:P * (p + 1)], qt[:, 2 * head + p, META:KV0],
                                    keys_t[:, 2 * head + p, :], start=True, stop=True)
                last.then_inc(S(tag + "_scores_done"), 1)

            if layer == 0:
                pe.wait_ge(S("rept_ready"), 1)
            pe.wait_ge(S(f"peer_wq{layer}_loaded"), 16)
            for hp in range(2 * PH):
                queries(hp)
                if hp == 1:
                    pe.wait_ge(S(tag + "_keys_out"), 4)
                    pe.sem_inc(S(f"v_used{layer}"), V_EARLY)
                    pe_transposes(pe, X_TILES[1:], tag, len(tiles))
                if hp >= 2 and hp % 2 == 0:
                    scores_of(hp // 2 - 1)
            scores_of(PH - 1)
            if layer == 0:
                pe.wait_ge(S(tag + "_scores_out"), PH)
                for p in range(2):
                    for head in range(PH):
                        last = m.matmul(bank(0)[:, P * p:P * (p + 1)], q_meta[:, p, head, :], keys_t[:, 2 * head + p, :],
                                        start=(head == 0), stop=(head == PH - 1))
                last.then_inc(S(tag + "_scores_done"), 1)
            pe.wait_ge(S(tag + "_scores_out"), PH + 1 - layer)
            pe.sem_inc(S(f"v_used{layer}"), RING - V_EARLY)
            pe.wait_ge(S(tag + "_t1_out"), 2)

        def peer_queries_act(act, layer, tag):
            a = nc.scalar
            c0 = META * layer
            if layer == 0:
                act.wait_ge(S("q_meta_zeroed"), 1)

            def scores_of(head):
                act.wait_ge(S(tag + "_scores_done"), head + 1)
                step(act, a.activation(scores[:, head, :], bank(head % 2)[:, 0:256], ACT.Copy), tag + "_scores_out")

            for hp in range(2 * PH):
                head = hp // 2
                act.wait_ge(S(tag + "_q_done"), hp + 1)
                if layer == 0:
                    step(act, a.activation(q_meta[:, hp % 2, head, META * head:META * (head + 1)],
                                           bank(4 + hp % 2)[:, 0:META], ACT.Copy), "q_meta_ready")
                step(act, a.activation(qt[:, hp, c0:KV0], bank(4 + hp % 2)[:, 0:KV0 - c0], ACT.Copy), tag + "_q_out")
                if hp >= 2 and hp % 2 == 0:
                    scores_of(head - 1)
            scores_of(PH - 1)
            if layer == 0:
                act.wait_ge(S(tag + "_scores_done"), PH + 1)
                step(act, a.activation(scores[:, META_UNIT, :], bank(0)[:, 0:256], ACT.Copy), tag + "_scores_out")

        def second_scores_pe(pe, layer, tag, head):
            m = nc.tensor
            pe.wait_ge(S(f"q1_copied{layer}"), head * 2 + 1)
            for k in range(KD):
                last = m.matmul(bank(4)[:, 0:256], hnt_x1[:, k, :], wq_peer[:, k, bass.ds(head * 256, 256)],
                                start=(k == 0), stop=(k == KD - 1))
            last.then_inc(S(f"q1_done{layer}"), 1)
            pe.wait_ge(S(f"q1_copied{layer}"), head * 2 + 2)
            for p in range(2):
                last = m.transpose(bank(5)[:, P * p:P * (p + 1)], q_rows[:, P * p:P * (p + 1)], ident[:])
            last.then_inc(S(f"q1_t{layer}"), 1)
            pe.wait_ge(S(f"q1_copied{layer}"), head * 2 + 3)
            pe.wait_ge(S(tag + "_scores_out"), head + unit_of(layer, 1, 0))
            for p in range(2):
                last = m.matmul(bank(5)[:, 256 + P * p:256 + P * (p + 1)].unsqueeze(1), q_cols[:, p, :],
                                keys_t[:, bass.ds(head * 2 + p, 1), :], start=True, stop=True)
            last.then_inc(S(f"scores1_done{layer}"), 1)

        def second_scores_act(act, layer, tag, head):
            a = nc.scalar
            act.wait_ge(S(f"q1_done{layer}"), head + 1)
            a.activation(q_rows, bank(4)[:, 0:256], ACT.Copy).then_inc(S(f"q1_copied{layer}"), 1)
            act.wait_ge(S(f"q1_t{layer}"), head + 1)
            a.activation(q_cols, cut(bank(5), 0, 2, P), ACT.Copy).then_inc(S(f"q1_copied{layer}"), 1)
            act.wait_ge(S(f"scores1_done{layer}"), head + 1)
            passed(act)
            a.activation(scores[:, bass.ds(head + unit_of(layer, 1, 0), 1), :], cut(bank(5), 256, 1, 256), ACT.Copy)\
                .then_inc(S(tag + "_scores_out"), 1)

        def peer_keys_dve(dve, layer, tag):
            v = nc.vector
            if layer == 0:
                dve.wait_ge(S("rep_t"), 1)
                step(dve, v.tensor_copy(rept[:], bank(5)[:, 0:META]), "rept_ready")
            for j in range(4):
                dve.wait_ge(S(tag + "_keys_t"), j + 1)
                step(dve, v.tensor_copy(keys_t[:, 4 * j:4 * j + 4, :], cut(bank(j), 0, 4, P)), tag + "_keys_out")

        def route(dve, layer, u, par):
            v = nc.vector
            w0, w1, w2 = (work[:, i, :] for i in range(3))

            def done(instruction):
                dve.drain()

            def top16(values, at, source, rest):
                done(v.max(values[:, 0:8], source))
                done(v.max_index(at[:, 0:8], values[:, 0:8], source))
                done(v.match_replace(rest, values[:, 0:8], source, MASKED))
                done(v.max(values[:, 8:16], rest))
                done(v.max_index(at[:, 8:16], values[:, 8:16], rest))

            done(v.tensor_copy(w0.unsqueeze(1), scores[:, bass.ds(u, 1), :]))
            for p in range(2):
                top16(half_v[:, p, :], half_i[:, p, :], w0[:, P * p:P * (p + 1)], w1[:, P * p:P * (p + 1)])
            v.tensor_scalar(half_f[:, 0, :], half_i[:, 0, :], float(KEYS), float(layer * EXPERTS), ALU.mult, ALU.add)
            v.tensor_copy(half_f[:, 1, :], half_i[:, 1, :])
            square = [P, TOPK, TOPK]
            sums = w2.rearrange("p (i j) -> p i j", i=TOPK)
            done(v.tensor_tensor(sums, half_v[:, 0, :].unsqueeze(2).broadcast_to(square),
                                 half_v[:, 1, :].unsqueeze(1).broadcast_to(square), ALU.add))
            top16(best[:, par, :], best_at[:], w2, w0)
            v.tensor_scalar(neg_best[:, par:par + 1], best[:, par, 0:1], -1.0, None, ALU.mult)\
                .then_inc(S(f"best_ready{layer}"), 1)
            v.tensor_scalar(ints[:, 0, :], best_at[:].bitcast(I32), 4, None, ALU.logical_shift_right)
            done(v.tensor_scalar(ints[:, 1, :], best_at[:].bitcast(I32), TOPK - 1, None, ALU.bitwise_and))
            done(v.tensor_copy(pos_f[:], ints[:]))
            for p, w in enumerate((w0, w1)):
                onehot = w.rearrange("p (i j) -> p i j", i=TOPK)
                done(v.tensor_tensor(onehot, pos_f[:, p, :].unsqueeze(2).broadcast_to(square),
                                     iota16[:].unsqueeze(1).broadcast_to(square), ALU.is_equal))
                done(v.tensor_tensor(onehot, onehot, half_f[:, p, :].unsqueeze(1).broadcast_to(square), ALU.mult))
                done(v.tensor_reduce(picked[:, p, :], onehot, X, ALU.add))
            done(v.tensor_tensor(expert[:, par, :], picked[:, 0, :], picked[:, 1, :], ALU.add)
                 .then_inc(S(f"experts_ready{layer}"), 1))

        def gathers(pool, layer, u, par):
            tables = (("u", ring_u, peer_u, "dots_done"), ("v", ring_v, peer_v, "v_used"))
            pool.wait_ge(S(f"experts_ready{layer}"), u + 1)
            passed(pool)
            for name, ring, table, freed in tables:
                rows = table.rearrange("l e d -> (l e) d")
                for k in range(TOPK):
                    pool.wait_ge(S(f"{freed}{layer}"), u * TOPK + (k + 1))
                    passed(pool)
                    nc.gpsimd.indirect_dma_start(
                        out=ring[k % RING], out_offset=None, in_=rows,
                        in_offset=bass.IndirectOffsetOnAxis(ap=expert[:, par, k:k + 1], axis=0))\
                        .then_inc(S(f"{name}{k % RING}_loaded{layer}"), 16)

        def unit_dots(dve, layer, u, par, rows):
            v = nc.vector
            for k in range(TOPK):
                dve.wait_ge(S(f"u{k % RING}_loaded{layer}"), u * 32 + 16 * (k // RING + 1))
                v.tensor_tensor_reduce(out=ring_u[k % RING], in0=ring_u[k % RING], in1=rows, scale=1.0, scalar=0.0,
                                       op0=ALU.mult, op1=ALU.add, accum_out=dots[:, par, k:k + 1])\
                    .then_inc(S(f"dots_done{layer}"), 1)
            dve.wait_ge(S(f"gelu_done{layer}"), u + 1)
            v.reciprocal(gate_sum[:, par:par + 1], gate_sum[:, par:par + 1])
            dve.drain()
            v.scalar_tensor_tensor(weight[:, par, :], dots[:, par, :], gate_sum[:, par:par + 1], gate[:, par, :],
                                   ALU.mult, ALU.mult).then_inc(S(f"weights_ready{layer}"), 1)

        def unit_act(act, layer, u, par, base, cols, meanwhile):
            a = nc.scalar
            act.wait_ge(S(f"best_ready{layer}"), u + 1)
            a.activation(gate[:, par, :], best[:, par, :], ACT.Exp, bias=neg_best[:, par:par + 1],
                         accum_out=gate_sum[:, par:par + 1])
            meanwhile()
            act.wait_ge(S(f"dots_done{layer}"), u * TOPK + (RING + TOPK))
            a.activation(dots[:, par, :], dots[:, par, :], ACT.Gelu).then_inc(S(f"gelu_done{layer}"), 1)
            act.wait_ge(S(f"weights_ready{layer}"), u + 1)
            for k in range(TOPK):
                act.wait_ge(S(f"v_used{layer}"), u * TOPK + (k + 1 + RING - DIAGS))
                a.activation(diag[:, k % DIAGS, 0:cols], base, ACT.Copy, scale=weight[:, par, k:k + 1])\
                    .then_inc(S(f"diag_ready{layer}"), 1)

        def unit_pe(pe, layer, u, y, cols):
            for k in range(TOPK):
                pe.wait_ge(S(f"v{k % RING}_loaded{layer}"), u * 32 + 16 * (k // RING + 1))
                pe.wait_ge(S(f"diag_ready{layer}"), u * TOPK + (k + 1))
                for half in range(2):
                    last = nc.tensor.matmul(y[:, BANK * half:BANK * (half + 1)], diag[:, k % DIAGS, 0:cols],
                                            ring_v[k % RING][:, BANK * half:BANK * (half + 1)], start=False, stop=False)
                last.then_inc(S(f"v_used{layer}"), 1)

        rows_x, rows_m = bank(2, 2), bank(6, 2)
        y_m = bank(4, 2)[0:META]
        y_x = [[bank(0, 2), bank(0, 2)], [bank(0, 2), bank(4, 2)]]
        LAST = 6

        def x_units(engine, layer, tile, unit):
            base = unit_of(layer, tile, 0)
            looped = PH - (LAST if layer == 0 and tile == NT - 1 else 0)
            with engine.Fori(0, looped // 2) as pair:
                for j in range(2):
                    unit(base + pair * 2 + j, (base + j) % 2, None)
            for j in range(looped, PH):
                unit(base + j, (base + j) % 2, j - looped)

        def peer_gpsimd(pool, layer, tag):
            pool.wait_ge(S(tag + "_keys_t"), 4)
            for tile in range(NT):
                x_units(pool, layer, tile, lambda u, par, j: gathers(pool, layer, u, par))
                if layer == 0 and tile == 0:
                    gathers(pool, layer, META_UNIT, 0)

        def peer_vector(dve, layer, tag):
            def next_route(u, par):
                dve.wait_ge(S(f"v_used{layer}"), u * TOPK + RING)
                passed(dve)
                dve.wait_ge(S(tag + "_scores_out"), u + 2)
                passed(dve)
                route(dve, layer, u + 1, 1 - par)

            def unit(u, par, j):
                unit_dots(dve, layer, u, par, rows_x)
                if j != LAST - 1:
                    next_route(u, par)
                if j is not None:
                    (dve_kv0_normed, dve_kv0_inputs, dve_k0, dve_k0, dve_k0, dve_nothing)[j](dve, j)

            dve.sem_inc(S(f"dots_done{layer}"), RING)
            dve.wait_ge(S(tag + "_scores_out"), 1)
            passed(dve)
            route(dve, layer, 0, 0)
            for tile in range(NT):
                nc.vector.tensor_copy(rows_x, hn[:, tile, :])
                dve.drain()
                x_units(dve, layer, tile, unit)
                if layer == 0 and tile == 0:
                    dve.wait_ge(S("meta_rows"), 2)
                    unit_dots(dve, layer, META_UNIT, 0, rows_m)
                    next_route(META_UNIT, 0)

        def peer_scalar(act, layer, tag):
            a = nc.scalar
            act.sem_inc(S(f"q1_copied{layer}"), 1)

            tiles_out = 0
            for tile in range(NT):
                def unit(u, par, j):
                    def beside():
                        if tile == 0:
                            second_scores_act(act, layer, tag, u)
                        elif j is not None:
                            ((act_kv0_norm, act_nothing) + (act_kv0,) * 4)[j](act, j)

                    unit_act(act, layer, u, par, ident[:], P, beside)

                x_units(act, layer, tile, unit)
                if layer == 1 and tile == 0:
                    act.sem_inc(S(tag + "_scores_out"), 1)
                tiles_out += 1
                act.wait_ge(S(f"y_closed{layer}"), tiles_out)
                a.activation(h[:, tile, :], y_x[layer][tile], ACT.Copy).then_inc(S(f"tile_out{layer}"), 1)
                if layer == 0 and tile == 0:
                    unit_act(act, layer, META_UNIT, 0, rept[:], META, lambda: None)
                    tiles_out += 1
                    act.wait_ge(S(f"y_closed{layer}"), tiles_out)
                    a.activation(h[0:META, NT, :], y_m, ACT.Copy).then_inc(S(f"tile_out{layer}"), 1)

        def peer_tensor(pe, layer, tag):
            m = nc.tensor

            def close(y, cols):
                for half in range(2):
                    last = m.matmul(y[:, BANK * half:BANK * (half + 1)].rearrange("p (a n) -> p a n", a=4),
                                    zeros[:, 0:cols], zeros[:].unsqueeze(1).broadcast_to([P, 4, P]),
                                    start=False, stop=True)
                last.then_inc(S(f"y_closed{layer}"), 1)

            for tile in range(NT):
                def unit(u, par, j):
                    if tile == 0:
                        second_scores_pe(pe, layer, tag, u)
                    elif j is not None:
                        ((pe_nothing, pe_kv0_transposes) + (pe_kv0,) * 4)[j](pe, j)
                    unit_pe(pe, layer, u, y_x[layer][tile], P)

                if tile == 1:
                    pe.wait_ge(*((S("tile_out0"), 1) if layer == 0 else (S(tag + "_scores_out"), NT * PH)))
                for half in range(2):
                    m.matmul(y_x[layer][tile][:, BANK * half:BANK * (half + 1)], ident[:],
                             h[:, tile, BANK * half:BANK * (half + 1)], start=True, stop=False)
                x_units(pe, layer, tile, unit)
                close(y_x[layer][tile], P)
                if layer == 0 and tile == 0:
                    pe.wait_ge(S(tag + "_scores_out"), NT * PH + 1)
                    for half in range(2):
                        m.matmul(y_m[:, BANK * half:BANK * (half + 1)], ident[0:META, 0:META],
                                 h[0:META, NT, BANK * half:BANK * (half + 1)], start=True, stop=False)
                    unit_pe(pe, layer, META_UNIT, y_m, META)
                    close(y_m, META)

        def kq(tag, n):
            if tag == "k0":
                room = [ua[:, KD * (L + KV0) + KV0 * i:KD * (L + KV0) + KV0 * (i + 1)] for i in range(5)]
                return kv_in0, wkv, k_t[:, n, 0:KV0], KV0, bank(4 + n % 3), bank(7), room
            room = [sc[:, KD * (T + P) + T * i:KD * (T + P) + T * (i + 1)] for i in range(4)]
            if n < KD:
                return kv_in1, wkv, k_t[:, n, KV0:L], P, bank(5 + n % 3), bank(n % 2), room
            return q_in, wq_att, q_t[:, n - KD, :], T, bank(5 + n % 3), bank(n % 2), room

        def kq_project(pe, tag, n):
            src, w, _, width, to, _, _ = kq(tag, n)
            if n >= 3:
                pe.wait_ge(S(tag + "_out"), n - 2)
            for k in range(KD):
                last = nc.tensor.matmul(to[:, 0:width], w[:, k, P * (n % KD):P * (n % KD + 1)], src[:, k, :],
                                        start=(k == 0), stop=(k == KD - 1))
            last.then_inc(S(tag + "_done"), 1)

        def kq_mean(pe, tag, n):
            _, _, _, width, _, to, room = kq(tag, n)
            held = 1 if tag == "k0" else 2
            if n >= held:
                pe.wait_ge(S(tag + "_roots"), n + 1 - held)
            pe.wait_ge(S(tag + "_squares"), n + 1)
            nc.tensor.matmul(to[:, 0:width], group_mean[:], room[n % 2][:, 0:width], start=True, stop=True)\
                .then_inc(S(tag + "_means"), 1)

        def kq_square(act, tag, n):
            _, _, _, width, product, _, room = kq(tag, n)
            act.wait_ge(S(tag + "_done"), n + 1)
            step(act, nc.scalar.activation(room[n % 2][:, 0:width], product[:, 0:width], ACT.Square), tag + "_squares")

        def kq_root(act, tag, n):
            _, _, _, width, _, means, room = kq(tag, n)
            act.wait_ge(S(tag + "_means"), n + 1)
            held = 3 if tag == "k0" else 2
            if n >= held:
                act.wait_ge(S(tag + "_out"), n + 1 - held)
            step(act, nc.scalar.activation(room[2 + n % held][:, 0:width], means[:, 0:width], ACT.Sqrt, bias=eps_col[:]),
                 tag + "_roots")

        def kq_out(dve, tag, n):
            _, _, to, width, product, _, room = kq(tag, n)
            dve.wait_ge(S(tag + "_roots"), n + 1)
            r = room[2 + n % (3 if tag == "k0" else 2)][:, 0:width]
            col = V_K if n < KD else V_Q
            step(dve, nc.vector.reciprocal(r, r), "dve_order")
            step(dve, nc.vector.scalar_tensor_tensor(to, product[:, 0:width], vec[:, col:col + 1], r,
                                                     ALU.mult, ALU.mult), tag + "_out")

        def kv_inputs(dve, tiles, tag):
            for n, psum, k, blocks, at, cols in transposed(tiles, tag):
                dve.wait_ge(S(tag + "_t"), n + 1)
                to, col = (kv_in0, at) if tag == "kv0" else (kv_in1, 0)
                uses = [(to, G_KV, col)] + ([(q_in, G_MIX1, at - META)] if cols == P else [])
                for to, gains, col in uses:
                    gain = vec[:, gains + k:gains + k + blocks].unsqueeze(2).broadcast_to([P, blocks, cols])
                    step(dve, nc.vector.tensor_tensor(to[:, k:k + blocks, col:col + cols], psum, gain, ALU.mult),
                         tag + "_t_out")

        def v_product(pe, src, rows, half, to, signal):
            for k in range(KD):
                last = nc.tensor.matmul(to[0:rows], src[:, k, :], wkv[:, k, D + BANK * half:D + BANK * (half + 1)],
                                        start=(k == 0), stop=(k == KD - 1))
            last.then_inc(S(signal), 1)

        KV0_TILES = [(P, 0, META), (META, NT, 0)]

        K0_PARTS = {2: range(0, 3), 3: range(3, 6), 4: range(6, KD), 5: range(0)}
        V0_PARTS = {2: (META, 0, kv_in0[:, :, 0:META], v_meta), 3: (META, 1, kv_in0[:, :, 0:META], v_meta),
                    4: (P, 0, kv_in0[:, :, META:KV0], hn[:, 0, :]), 5: (P, 1, kv_in0[:, :, META:KV0], hn[:, 0, :])}

        def dve_nothing(dve, j):
            pass

        act_nothing = pe_nothing = dve_nothing

        def act_kv0_norm(act, j):
            act_squares(act, KV0_TILES, "tile_out0", "kv0")

        def dve_kv0_normed(dve, j):
            for n, (rows, t, _) in enumerate(KV0_TILES):
                dve_inverse_rms(dve, n, rows, t, "kv0")
                step(dve, nc.vector.tensor_scalar(normed(t, "kv0")[0:rows], h[0:rows, t, :],
                                                  stats[0:rows, 9 + t:10 + t], None, ALU.mult), "kv0_normed")

        def pe_kv0_transposes(pe, j):
            pe_transposes(pe, KV0_TILES, "kv0")

        def dve_kv0_inputs(dve, j):
            kv_inputs(dve, KV0_TILES, "kv0")

        def pe_kv0(pe, j):
            if j == 2:
                pe.wait_ge(S("kv0_t_out"), 5)
                pe.wait_ge(S("w_kv_loaded"), 16)
            else:
                pe.wait_ge(S("v0_out"), j - 2)
            for n in K0_PARTS[j]:
                kq_project(pe, "k0", n)
                if n > K0_PARTS[j][0]:
                    kq_mean(pe, "k0", n - 1)
            if K0_PARTS[j]:
                kq_mean(pe, "k0", n)
                pe.wait_ge(S("k0_roots"), n + 1)
            rows, half, src, _ = V0_PARTS[j]
            v_product(pe, src, rows, half, bank(7), "v0_done")

        def act_kv0(act, j):
            for n in K0_PARTS[j]:
                kq_square(act, "k0", n)
                if n > K0_PARTS[j][0]:
                    kq_root(act, "k0", n - 1)
            if K0_PARTS[j]:
                kq_root(act, "k0", n)
            rows, half, _, to = V0_PARTS[j]
            act.wait_ge(S("v0_done"), j - 1)
            step(act, nc.scalar.activation(to[:, BANK * half:BANK * (half + 1)], bank(7)[0:rows], ACT.Copy), "v0_out")

        def dve_k0(dve, j):
            for n in K0_PARTS[j]:
                kq_out(dve, "k0", n)

        with nc.Block(no_gpsimd_drain=True) as block:
            @block.sync
            def _(sp):
                sp.dma_start(h[:, 0:NT, :], x[0].rearrange("(t p) d -> p t d", p=P)).then_inc(S("x_loaded"), 16)
                rows = [(conf_dw_w[0], CONF_K), (sconv_w[0], SC_K), (lru_conv_w[0], LRU_K), (conf_dw_b, 1),
                        (conf_gn_g, 1), (conf_gn_b, 1), (lru_conv_b, 1), (lru_ba, 1), (lru_bx, 1), (lru_lam, 1)]
                at = 0
                for v, n in rows:
                    sp.dma_start(vrows[at:at + n * NC, :], v.rearrange("k (c p) -> (k c) p", p=P))\
                        .then_inc(S("vectors_loaded"), 16)
                    at += n * NC
                gains = [pre_mix_g, pre_mlp_g, norm_mix[0:1], kv_norm.rearrange("(o n) -> o n", o=1), norm_mix[1:2]]
                for i, v in enumerate(gains):
                    sp.dma_start(grows[KD * i:KD * (i + 1), :], v.rearrange("o (k p) -> (o k) p", p=P))\
                        .then_inc(S("vectors_loaded"), 16)
                k_row = k_norm.rearrange("(o n) -> o n", o=1)
                for i, v in enumerate((k_row, q_norm)):
                    for half in range(2):
                        sp.dma_start(grows[V_GAIN + i:V_GAIN + i + 1, HD * half:HD * (half + 1)], v)\
                            .then_inc(S("vectors_loaded"), 16)
                w_in_v = w_in[0].rearrange("(k p) n -> p k n", p=P)
                for c in range(5):
                    sp.dma_start(win[c], w_in_v[:, :, CHUNK * c:CHUNK * (c + 1)]).then_inc(S(f"w_in{c}_loaded"), 16)
                sp.wait_ge(S("constants_ready"), 8)
                for w, blocks in enumerate((lru_wa, lru_wx)):
                    for g in range(2 * NC):
                        r = HD * (g % 2)
                        sp.dma_start(bd[r:r + HD, w, g // 2, r:r + HD], blocks[0, g]).then_inc(S("lru_w_loaded"), 16)
                sp.dma_start(wout, w_out[0].rearrange("(k p) n -> p k n", p=P)).then_inc(S("w_out_loaded"), 16)
                sp.dma_start(gb[:, 0, :], post_mix_g[0].partition_broadcast(P)).then_inc(S("gain0_loaded"), 16)
                sp.dma_start(h[0:META, NT, :], meta_tokens).then_inc(S("meta_loaded"), 16)
                sp.wait_ge(S("u_done"), 10)
                w1_v = mlp_w1[0].rearrange("(k p) n -> p k n", p=P)
                w2_v = mlp_w2[0].rearrange("(f p) n -> p f n", p=P)
                for c in range(2):
                    sp.dma_start(w1b[c], w1_v[:, :, CHUNK * c:CHUNK * (c + 1)]).then_inc(S(f"w1_{c}_loaded"), 16)
                sp.dma_start(w2b[0], w2_v[:, 0:FT, :]).then_inc(S("w2_0_loaded"), 16)
                sp.wait_ge(S("vectors_t"), 1)
                sp.dma_start(gb[:, 1, :], post_mlp_g[0].partition_broadcast(P)).then_inc(S("gain1_loaded"), 16)

            @block.gpsimd
            def _(pool):
                g = nc.gpsimd

                def const(instruction):
                    step(pool, instruction, "constants_ready")

                const(g.memset(ident[:], 0.0))
                const(g.affine_select(out=ident[:], in_=ident[:], compare_op=ALU.not_equal, fill=1.0, base=0,
                                      pattern=[[-1, P]], channel_multiplier=1))
                const(g.memset(zpad[:, :, 0:CONF_K - 1], 0.0))
                const(g.memset(spad[:, :, 0:SC_K - 1], 0.0))
                const(g.memset(xpad[:, :, 0:LRU_K - 1], 0.0))
                const(g.memset(zeros[:], 0.0))
                const(g.memset(group_mean[:], 0.0))
                const(g.memset(bd, 0.0))
                for i in range(2):
                    const(g.memset(group_mean[HD * i:HD * (i + 1), HD * i:HD * (i + 1)], 1.0 / HD))
                const(g.iota(alibi_i[:, 0:P], [[-1, P]], base=0, channel_multiplier=1))
                const(g.iota(alibi_i[:, P:384], [[-1, T]], base=P, channel_multiplier=1))
                for a in range(ATT_H):
                    const(g.tensor_copy(alibi[:, a, :], alibi_i))
                    const(g.tensor_scalar(alibi[:, a, :], alibi[:, a, :], -(2.0 ** (-8.0 * (a + 1) / ATT_H)), None,
                                          ALU.mult))
                    for lo, n, base in ((0, P, 0), (P, T, P)):
                        const(g.affine_select(out=alibi[:, a, lo:lo + n], in_=alibi[:, a, lo:lo + n],
                                              compare_op=ALU.is_ge, fill=NEG, base=base, pattern=[[-1, n]],
                                              channel_multiplier=1))
                const(g.iota(ratio_i[:], [[1, META]], base=1, channel_multiplier=0))
                const(g.iota(iota16_i[:], [[1, TOPK]], base=0, channel_multiplier=0))
                const(g.memset(eps_col[:], EPS))
                const(g.memset(rep[:], 0.0))
                const(g.affine_select(out=rep[:], in_=rep[:], compare_op=ALU.not_equal, fill=1.0, base=0,
                                      pattern=[[0, PH], [-1, META]], channel_multiplier=1))

            @block.scalar
            def _(act):
                a = nc.scalar

                act.wait_ge(S("x_loaded"), 16)
                for t in range(NT):
                    step(act, a.activation(ua[:, 0:D], h[:, t, :], ACT.Square, accum_out=stats[:, t:t + 1]), "x_squares")
                act.wait_ge(S("x_var"), 1)
                step(act, a.activation(stats[:, 4:6], stats[:, 2:4], ACT.Sqrt), "x_std")
                act.wait_ge(S("lam_abs"), 1)
                step(act, a.activation(lam[3], lam[1], ACT.Exp, scale=-1.0), "lam_exp")
                act.wait_ge(S("lam_one"), 1)
                step(act, a.activation(lam[5], lam[4], ACT.Ln), "lam_ln")
                act.wait_ge(S("u_done"), 2)
                step(act, a.activation(sg, cut(bank(5), 0, NC, T), ACT.Sigmoid), "u_out")
                for pair, b, to in ((2, 6, ub), (3, 7, uc), (5, 1, uq), (6, 2, uk), (7, 3, uv)):
                    act.wait_ge(S("u_done"), pair + 1)
                    step(act, a.activation(to, cut(bank(b), 0, NC, T), ACT.Copy), "u_out")
                act.wait_ge(S("u_done"), 9)
                act.wait_ge(S("constants_ready"), 5)
                step(act, a.activation(xpad[:, :, LRU_K - 1:], cut(bank(6), 0, NC, T), ACT.Copy), "u_out")
                act.wait_ge(S("gn_var"), 1)
                step(act, a.activation(uc, sg, ACT.Sqrt), "gn_std")
                act.wait_ge(S("u_done"), 10)
                step(act, a.activation(gg, cut(bank(7), 0, NC, T), ACT.Gelu_apprx_tanh), "u_out")
                for head in range(ATT_H):
                    act.wait_ge(S("att_max"), 2 * head + 2)
                    for t, (lo, n) in enumerate(((0, P), (P, T))):
                        step(act, a.activation(soft[:, head, lo:lo + n], soft[:, head, lo:lo + n], ACT.Exp,
                                               bias=att_m[:, 2 * head + t:2 * head + t + 1],
                                               accum_out=att_s[:, 2 * head + t:2 * head + t + 1]), "att_exp")
                act.wait_ge(S("lru_gates_done"), 2)
                for w, (to, bias) in enumerate(((r_s, V_BA), (i_s, V_BX))):
                    for c in range(NC):
                        step(act, a.activation(to[:, c], bank(4 + w)[:, T * c:T * (c + 1)], ACT.Sigmoid,
                                               bias=vec[:, bias + c:bias + c + 1]), "lru_sigmoid")
                act.wait_ge(S("gn_out"), NC)
                step(act, a.activation(yt[:, 0:NC], gd, ACT.Silu), "y_a")
                act.wait_ge(S("lru_log"), NC)
                step(act, a.activation(a_s, r_s, ACT.Exp), "lru_a")
                step(act, a.activation(th_s, r_s, ACT.Tanh, scale=-1.0), "lru_a")
                act.wait_ge(S("lru_sq"), 1)
                step(act, a.activation(th_s, th_s, ACT.Sqrt), "lru_mult")
                act.wait_ge(S("att_pv"), 1)
                step(act, a.activation(yt[:, 4:6], cut(bank(6), 0, NC, T), ACT.Copy), "y_c")
                act.wait_ge(S("constants_ready"), 31)
                for t in range(NT):
                    act.wait_ge(S("y_done"), t + 1)
                    step(act, a.activation(ua[:, 0:D], bank(2 * t, 2), ACT.Square, accum_out=stats[:, t:t + 1]), "y_squares")
                    act_root_mean(act, P, t, "y")
                for t in range(NT):
                    act.wait_ge(S("x1"), t + 1)
                    step(act, a.activation(ua[:, 0:D], h[:, t, :], ACT.Square, accum_out=stats[:, t:t + 1]), "x1_squares")
                    act_root_mean(act, P, t, "x1")

            @block.vector
            def _(dve):
                v = nc.vector

                def chain(instruction):
                    step(dve, instruction, "dve_order")

                def rms(squares, var, std):
                    dve.wait_ge(S(squares), NT)
                    step(dve, v.tensor_scalar(stats[:, 2:4], stats[:, 0:2], 1.0 / D, EPS, ALU.mult, ALU.add), var)
                    dve.wait_ge(S(std), 1)
                    chain(v.reciprocal(stats[:, 6:8], stats[:, 4:6]))

                rms("x_squares", "x_var", "x_std")
                for t in range(NT):
                    step(dve, v.tensor_scalar(hn[:, t, :], h[:, t, :], stats[:, 6 + t:7 + t], None, ALU.mult), "x_normed")
                dve.wait_ge(S("vectors_t"), 1)
                chain(v.tensor_copy(vec[:, 0:V_CHAN], bank(7)[:, 0:V_CHAN]))
                step(dve, v.tensor_copy(vec[:, V_CHAN:VECS], bank(7)[:, P:P + VECS - V_CHAN]), "vectors_ready")
                for t in range(NT):
                    dve.wait_ge(S("x_t"), t + 1)
                    for j in range(2):
                        gain = vec[:, G_PREMIX + 4 * j:G_PREMIX + 4 * j + 4].unsqueeze(2).broadcast_to([P, 4, P])
                        step(dve, v.tensor_tensor(ht[:, 4 * j:4 * j + 4, P * t:P * (t + 1)],
                                                  cut(bank(2 * t + j), 0, 4, P), gain, ALU.mult), "h_t")
                lamv = vec[:, V_LAM:V_LAM + NC]
                chain(v.tensor_scalar(lam[0], lamv, -1.0, 0.0, ALU.mult, ALU.max))
                chain(v.tensor_scalar(lam[1], lamv, -1.0, None, ALU.mult))
                step(dve, v.tensor_tensor(lam[1], lam[1], lamv, ALU.max), "lam_abs")
                dve.wait_ge(S("lam_exp"), 1)
                step(dve, v.tensor_scalar(lam[4], lam[3], 1.0, None, ALU.add), "lam_one")
                chain(v.tensor_scalar(lam[1], lam[4], -1.0, None, ALU.add))
                chain(v.tensor_tensor(lam[1], lam[3], lam[1], ALU.subtract))
                chain(v.reciprocal(lam[2], lam[4]))
                chain(v.tensor_tensor(lam[1], lam[1], lam[2], ALU.mult))
                chain(v.tensor_tensor(lam[0], lam[0], lam[1], ALU.add))
                dve.wait_ge(S("lam_ln"), 1)
                chain(v.tensor_tensor(lam[0], lam[0], lam[5], ALU.add))
                chain(v.tensor_scalar(lam8[:], lam[0], -LRU_C, None, ALU.mult))
                dve.wait_ge(S("u_done"), 1)
                dve.wait_ge(S("u_out"), 1)
                dve.wait_ge(S("constants_ready"), 5)
                chain(v.tensor_tensor(zpad[:, :, CONF_K - 1:], cut(bank(4), 0, NC, T), sg, ALU.mult))
                for c in range(NC):
                    chain(v.tensor_scalar(conv[:, c], zpad[:, c, 0:T], vec[:, V_CONF + c:V_CONF + c + 1],
                                          vec[:, V_DWB + c:V_DWB + c + 1], ALU.mult, ALU.add))
                with dve.Fori(1, CONF_K) as tap:
                    for c in range(NC):
                        v.scalar_tensor_tensor(conv[:, c], zpad[:, c, bass.ds(tap, T)],
                                               vec[:, bass.ds(tap * NC + (V_CONF + c), 1)], conv[:, c],
                                               ALU.mult, ALU.add)
                    dve.drain()
                dve.drain().then_inc(S("conv_done"), 1)
                dve.wait_ge(S("u_done"), 5)
                dve.wait_ge(S("u_out"), 3)
                step(dve, v.tensor_tensor(spad[:, :, SC_K - 1:], cut(bank(0), 0, NC, T), uc, ALU.mult), "xs_used")
                for c in range(NC):
                    chain(v.tensor_scalar(uc[:, c], spad[:, c, 0:T], vec[:, V_SC + c:V_SC + c + 1], None, ALU.mult))
                for tap in range(1, SC_K):
                    for c in range(NC):
                        col = V_SC + tap * NC + c
                        chain(v.scalar_tensor_tensor(uc[:, c], spad[:, c, tap:tap + T], vec[:, col:col + 1], uc[:, c],
                                                     ALU.mult, ALU.add))
                dve.wait_ge(S("gn_mean"), 1)
                chain(v.tensor_tensor(gd, conv, cut(bank(4), 0, NC, T), ALU.subtract))
                step(dve, v.tensor_tensor(sg, gd, gd, ALU.mult), "gn_sq")
                step(dve, v.tensor_tensor(yt[:, 2:4], ub, uc, ALU.mult), "y_b")
                dve.wait_ge(S("gn_var_done"), 1)
                step(dve, v.tensor_scalar(sg, cut(bank(5), 0, NC, T), GN_EPS, None, ALU.add), "gn_var")
                dve.wait_ge(S("u_out"), 7)
                for c in range(NC):
                    chain(v.tensor_scalar(xc[:, c], xpad[:, c, 0:T], vec[:, V_LRUW + c:V_LRUW + c + 1],
                                          vec[:, V_LRUB + c:V_LRUB + c + 1], ALU.mult, ALU.add))
                for tap in range(1, LRU_K):
                    for c in range(NC):
                        col = V_LRUW + tap * NC + c
                        step(dve, v.scalar_tensor_tensor(xc[:, c], xpad[:, c, tap:tap + T], vec[:, col:col + 1],
                                                         xc[:, c], ALU.mult, ALU.add), "lru_conv")
                for head in range(ATT_H):
                    dve.wait_ge(S("att_scores"), head + 1)
                    dve.wait_ge(S("constants_ready"), 28)
                    step(dve, v.scalar_tensor_tensor(soft[:, head, :], bank(head)[:, 0:384], HD ** -0.5,
                                                     alibi[:, head, :], ALU.mult, ALU.add), "att_biased")
                    for t, (lo, n) in enumerate(((0, P), (P, T))):
                        step(dve, v.tensor_reduce(att_m[:, 2 * head + t:2 * head + t + 1], soft[:, head, lo:lo + n], X,
                                                  ALU.max, negate=True), "att_max")
                dve.wait_ge(S("gn_std"), 1)
                chain(v.reciprocal(sg, uc))
                chain(v.tensor_tensor(gd, gd, sg, ALU.mult))
                for c in range(NC):
                    step(dve, v.tensor_scalar(gd[:, c], gd[:, c], vec[:, V_GNG + c:V_GNG + c + 1],
                                              vec[:, V_GNB + c:V_GNB + c + 1], ALU.mult, ALU.add), "gn_out")
                dve.wait_ge(S("att_exp"), 2 * ATT_H)
                chain(v.reciprocal(att_s[:], att_s[:]))
                for head in range(ATT_H):
                    for t, (lo, n) in enumerate(((0, P), (P, T))):
                        step(dve, v.tensor_scalar(soft[:, head, lo:lo + n], soft[:, head, lo:lo + n],
                                                  att_s[:, 2 * head + t:2 * head + t + 1], None, ALU.mult), "att_probs")
                dve.wait_ge(S("lru_sigmoid"), 2 * NC)
                for c in range(NC):
                    step(dve, v.tensor_scalar(r_s[:, c], r_s[:, c], lam8[:, c:c + 1], None, ALU.mult), "lru_log")
                chain(v.tensor_tensor(i_s, i_s, xc, ALU.mult))
                for head in range(ATT_H):
                    dve.wait_ge(S("att_probs_t"), head + 1)
                    step(dve, v.tensor_copy(probs_t[:, head, :], bank(head)[:, 0:384]), "att_probs_t_out")
                dve.wait_ge(S("lru_a"), 2)
                chain(v.tensor_tensor(b_s, a_s, a_s, ALU.mult))
                step(dve, v.scalar_tensor_tensor(th_s, b_s, 1.0, th_s, ALU.add, ALU.mult), "lru_sq")
                dve.wait_ge(S("lru_mult"), 1)
                chain(v.tensor_tensor(b_s, i_s, th_s, ALU.mult))
                for c in range(NC):
                    chain(v.tensor_tensor_scan(xc[:, c], a_s[:, c], b_s[:, c], 0.0, ALU.mult, ALU.add))
                dve.wait_ge(S("u_out"), 8)
                step(dve, v.tensor_tensor(yt[:, 6:8], xc, gg, ALU.mult), "y_d")
                dve.wait_ge(S("gain0_loaded"), 16)
                for t in range(NT):
                    dve_inverse_rms(dve, t, P, t, "y")
                    chain(v.scalar_tensor_tensor(tmp[:, t, :], bank(2 * t, 2), stats[:, 9 + t:10 + t], gb[:, 0, :],
                                                 ALU.mult, ALU.mult))
                    step(dve, v.tensor_tensor(h[:, t, :], h[:, t, :], tmp[:, t, :], ALU.add), "x1")
                for t in range(NT):
                    dve_inverse_rms(dve, t, P, t, "x1")
                    step(dve, v.tensor_scalar(hn[:, t, :], h[:, t, :], stats[:, 9 + t:10 + t], None, ALU.mult), "x1_normed")
                for t in range(NT):
                    dve.wait_ge(S("x1_t"), t + 1)
                    for j in range(2):
                        gain = vec[:, G_PREMLP + 4 * j:G_PREMLP + 4 * j + 4].unsqueeze(2).broadcast_to([P, 4, P])
                        step(dve, v.tensor_tensor(h2t[:, 4 * j:4 * j + 4, P * t:P * (t + 1)],
                                                  cut(bank(4 + 2 * t + j), 0, 4, P), gain, ALU.mult), "h2_t")

            @block.tensor
            def _(pe):
                m = nc.tensor
                pe.wait_ge(S("constants_ready"), 2)
                pe.wait_ge(S("x_normed"), NT)
                for t in range(NT):
                    for k in range(KD):
                        last = m.transpose(bank(2 * t + k // 4)[:, P * (k % 4):P * (k % 4 + 1)],
                                           hn[:, t, P * k:P * (k + 1)], ident[:])
                    last.then_inc(S("x_t"), 1)
                pe.wait_ge(S("vectors_loaded"), 16 * 19)
                m.transpose(bank(7)[:, 0:V_CHAN], vrows[0:V_CHAN, :], ident[0:V_CHAN, 0:V_CHAN])
                n = VECS - V_CHAN
                m.transpose(bank(7)[:, P:P + n], grows[0:n, :], ident[0:n, 0:n]).then_inc(S("vectors_t"), 1)
                pe.wait_ge(S("h_t"), 4)
                pe.wait_ge(S("vectors_ready"), 1)

                def project(pair, b):
                    chunk, at = pair // 2, (pair % 2) * 2
                    pe.wait_ge(S(f"w_in{chunk}_loaded"), 16)
                    for c in range(NC):
                        for k in range(KD):
                            last = m.matmul(bank(b)[:, T * c:T * (c + 1)],
                                            win[chunk][:, k, P * (at + c):P * (at + c + 1)],
                                            ht[:, k, :], start=(k == 0), stop=(k == KD - 1))
                    last.then_inc(S("u_done"), 1)

                for pair, b in ((0, 4), (1, 5), (2, 6), (3, 7), (4, 0), (5, 1), (6, 2)):
                    project(pair, b)
                for t in range(NT):
                    for k in range(KD):
                        last = m.matmul(bank(3)[:, T * t:T * (t + 1)], ht[:, k, P * t:P * (t + 1)],
                                        win[3][:, k, T:2 * T], start=(k == 0), stop=(k == KD - 1))
                last.then_inc(S("u_done"), 1)
                pe.wait_ge(S("u_out"), 3)
                project(8, 6)
                project(9, 7)
                pe.wait_ge(S("conv_done"), 1)
                pe.wait_ge(S("constants_ready"), 10)
                m.matmul(bank(4), group_mean[:], conv, start=True, stop=True).then_inc(S("gn_mean"), 1)
                pe.wait_ge(S("u_out"), 6)
                pe.wait_ge(S("xs_used"), 1)
                for head in range(ATT_H):
                    r, c = HD * (head % 2), head // 2
                    for t, (lo, n) in enumerate(((0, P), (P, T))):
                        last = m.matmul(bank(head)[:, lo:lo + n], uq[r:r + HD, c, P * t:P * (t + 1)],
                                        uk[r:r + HD, c, 0:n], start=True, stop=True)
                    last.then_inc(S("att_scores"), 1)
                pe.wait_ge(S("gn_sq"), 1)
                m.matmul(bank(5), group_mean[:], sg, start=True, stop=True).then_inc(S("gn_var_done"), 1)
                pe.wait_ge(S("lru_w_loaded"), 16 * 8)
                pe.wait_ge(S("lru_conv"), (LRU_K - 1) * NC)
                pe.wait_ge(S("gn_var"), 1)
                for w in range(2):
                    for c in range(NC):
                        last = m.matmul(bank(4 + w)[:, T * c:T * (c + 1)], bd[:, w, c, :], xc[:, c, :],
                                        start=True, stop=True)
                    last.then_inc(S("lru_gates_done"), 1)
                for head in range(ATT_H):
                    pe.wait_ge(S("att_probs"), 2 * head + 2)
                    for j in range(3):
                        last = m.transpose(bank(head)[:, P * j:P * (j + 1)], soft[:, head, P * j:P * (j + 1)], ident[:])
                    last.then_inc(S("att_probs_t"), 1)
                pe.wait_ge(S("u_out"), 7)
                for head in range(ATT_H):
                    pe.wait_ge(S("att_probs_t_out"), head + 1)
                    r, c = HD * (head % 2), head // 2
                    to = bank(6)[r:r + HD, T * c:T * (c + 1)]
                    m.matmul(to[:, 0:P], uv[:, 0, HD * head:HD * (head + 1)], probs_t[:, head, 0:P], start=True, stop=True)
                    m.matmul(to[:, P:T], uv[:, 0, HD * head:HD * (head + 1)], probs_t[:, head, P:T], start=True, stop=False)
                    last = m.matmul(to[:, P:T], uv[:, 1, HD * head:HD * (head + 1)], probs_t[:, head, T:384],
                                    start=False, stop=True)
                last.then_inc(S("att_pv"), 1)
                pe.wait_ge(S("w_out_loaded"), 16)
                for t, ks in ((0, (2, 3, 0, 1)), (1, (2, 3, 0, 1)), (0, (4, 5, 6, 7)), (1, (4, 5, 6, 7))):
                    for k in ks:
                        for first, signal in ((2, "y_b"), (0, "y_a"), (4, "y_c"), (6, "y_d")):
                            if k == first and t == 0:
                                pe.wait_ge(S(signal), 1)
                        for half in range(2):
                            last = m.matmul(bank(2 * t + half), yt[:, k, P * t:P * (t + 1)],
                                            wout[:, k, BANK * half:BANK * (half + 1)], start=(k == 2), stop=(k == 7))
                    if 7 in ks:
                        last.then_inc(S("y_done"), 1)
                for t in range(NT):
                    pe.wait_ge(S("x1_normed"), t + 1)
                    for k in range(KD):
                        last = m.transpose(bank(4 + 2 * t + k // 4)[:, P * (k % 4):P * (k % 4 + 1)],
                                           hn[:, t, P * k:P * (k + 1)], ident[:])
                    last.then_inc(S("x1_t"), 1)

        forget({"gain0_loaded", "gain1_loaded", "meta_loaded", "w1_0_loaded", "w1_1_loaded", "w2_0_loaded", "h2_t", "dve_order"})

        with nc.Block(no_gpsimd_drain=True) as block:
            @block.sync
            def _(sp):
                w1_v = mlp_w1[0].rearrange("(k p) n -> p k n", p=P)
                w2_v = mlp_w2[0].rearrange("(f p) n -> p f n", p=P)
                sp.dma_start(w2b[1], w2_v[:, FT:2 * FT, :]).then_inc(S("w2_1_loaded"), 16)
                sp.dma_start(gb[:, 0, :], pool_scale[0].partition_broadcast(P)).then_inc(S("gain0_loaded"), 16)
                with sp.Fori(0, DFF // CHUNK // 2 - 1) as i:
                    for b in range(2):
                        sp.wait_ge(S("up_done"), i * (2 * FT) + FT * (b + 1))
                        sp.dma_start(w1b[b], w1_v[:, :, bass.ds(i * (2 * CHUNK) + CHUNK * (b + 2), CHUNK)])\
                            .then_inc(S(f"w1_{b}_loaded"), 16)
                        sp.wait_ge(S("down_done"), i * (2 * FT) + FT * (b + 2))
                        sp.dma_start(w2b[b], w2_v[:, bass.ds(i * (2 * FT) + FT * (b + 2), FT), :])\
                            .then_inc(S(f"w2_{b}_loaded"), 16)
                sp.dma_start(wq_peer, peer_wq[0].rearrange("(k p) n -> p k n", p=P)).then_inc(S("peer_wq0_loaded"), 16)

            @block.scalar
            def _(act):
                a = nc.scalar
                act.sem_inc(S("up_bank_free"), FT)
                with act.Fori(0, DFF // CHUNK // 2) as i:
                    for q in range(2 * FT):
                        act.wait_ge(S("up_done"), i * (2 * FT) + (q + 1))
                        a.activation(relu[:, q % 2, :], bank(4 + q % FT)[:, 0:T], ACT.Relu)\
                            .then_inc(S("up_bank_free"), 1)
                        act.drain()
                        act.wait_ge(S("down_done"), i * (2 * FT) + (q + 1))
                        a.activation(act2[:, q % FT, :], relu[:, q % 2, :], ACT.Square).then_inc(S("hidden_ready"), 1)
                        act.drain()
                act.wait_ge(S("mlp_done"), 1)
                for t in range(NT):
                    step(act, a.activation(sc[:, 3072:3072 + D], bank(2 * t, 2), ACT.Square, accum_out=stats[:, t:t + 1]),
                         "m_squares")
                    act_root_mean(act, P, t, "m")

            @block.tensor
            def _(pe):
                m = nc.tensor

                def seed(b, start):
                    return m.matmul(cut(bank(b), 0, 4, P), zeros[:], zeros[:].unsqueeze(1).broadcast_to([P, 4, P]),
                                    start=start, stop=not start)

                for b in range(4):
                    last = seed(b, True)
                last.then_inc(S("down_done"), FT)
                pe.wait_ge(S("h2_t"), 4)
                with pe.Fori(0, DFF // CHUNK // 2) as i:
                    def up(q):
                        b = q // FT
                        if q % FT == 0:
                            pe.wait_ge(S(f"w1_{b}_loaded"), i * 16 + 16)
                        pe.wait_ge(S("up_bank_free"), i * (2 * FT) + (q + 1))
                        for k in range(KD):
                            last = m.matmul(bank(4 + q % FT)[:, 0:T], w1b[b][:, k, P * (q % FT):P * (q % FT + 1)],
                                            h2t[:, k, :], start=(k == 0), stop=(k == KD - 1))
                        last.then_inc(S("up_done"), 1)

                    def down(q):
                        b = q // FT
                        if q % FT == 0:
                            pe.wait_ge(S(f"w2_{b}_loaded"), i * 16 + 16)
                        pe.wait_ge(S("hidden_ready"), i * (2 * FT) + (q + 1))
                        for t in range(NT):
                            for half in range(2):
                                last = m.matmul(bank(2 * t + half), act2[:, q % FT, P * t:P * (t + 1)],
                                                w2b[b][:, q % FT, BANK * half:BANK * (half + 1)],
                                                start=False, stop=False)
                        last.then_inc(S("down_done"), 1)

                    up(0)
                    for q in range(2 * FT):
                        if q + 1 < 2 * FT:
                            up(q + 1)
                        down(q)
                for b in range(4):
                    last = seed(b, False)
                last.then_inc(S("mlp_done"), 1)

            @block.vector
            def _(dve):
                v = nc.vector
                step(dve, v.tensor_copy(iota16[:], iota16_i[:]), "dve_order")
                step(dve, v.tensor_copy(ratio[:, 0, :], ratio_i[:]), "dve_order")
                step(dve, v.reciprocal(ratio[:, 3, :], ratio[:, 0, :]), "dve_order")
                for g in range(POOL_GROUPS):
                    step(dve, v.tensor_scalar(ratio[:, g, :], ratio[:, 3, :], 2.0 ** (g + 1), 1.0, ALU.mult, ALU.max),
                         "ratio_ready")
                dve.wait_ge(S("gain1_loaded"), 16)
                for t in range(NT):
                    dve_inverse_rms(dve, t, P, t, "m")
                    step(dve, v.scalar_tensor_tensor(tmp[:, t, :], bank(2 * t, 2), stats[:, 9 + t:10 + t], gb[:, 1, :],
                                                     ALU.mult, ALU.mult), "dve_order")
                    step(dve, v.tensor_tensor(h[:, t, :], h[:, t, :], tmp[:, t, :], ALU.add), "x2")

        TILES = [X_TILES[0], META_TILE, X_TILES[1]]
        with nc.Block() as block:
            @block.sync
            def _(sp):
                sp.dma_start(gb[:, 1, :], norm_ffn[0].partition_broadcast(P)).then_inc(S("gain1_loaded"), 16)
                sp.dma_start(poolw, pool_w[0].rearrange("g (k p) n -> p (g k) n", p=P)).then_inc(S("pool_w_loaded"), 16)
                sp.dma_start(keys_in[0], peer_keys[0].rearrange("h w n c -> n (h w) c"))\
                    .then_inc(S("peer_keys0_loaded"), 16)
                sp.wait_ge(S("ffn0_scores_out"), NT * PH + 1)
                sp.dma_start(wkv, w_kv.rearrange("(k p) n -> p k n", p=P)).then_inc(S("w_kv_loaded"), 16)
                sp.dma_start(gb[:, 0, :], norm_ffn[1].partition_broadcast(P)).then_inc(S("gain0_loaded"), 16)

            @block.gpsimd
            def _(pool):
                for i in range(3):
                    nc.gpsimd.memset(seq[i][:, :, 0:META], 0.0).then_inc(S("pads_ready"), 1)
                pool.wait_ge(S("pooled"), 2 * POOL_GROUPS)
                nc.gpsimd.memset(q_meta, 0.0).then_inc(S("q_meta_zeroed"), 1)
                peer_gpsimd(pool, 0, "ffn0")

            @block.scalar
            def _(act):
                act.wait_ge(S("meta_loaded"), 16)
                act_squares(act, TILES, None, "pool")
                act_squares(act, TILES, "h1", "ffn0")
                peer_queries_act(act, 0, "ffn0")
                peer_scalar(act, 0, "ffn0")

            @block.vector
            def _(dve):
                v = nc.vector
                for n, (rows, t, _) in enumerate(TILES):
                    dve_inverse_rms(dve, n, rows, t, "pool")
                    step(dve, v.tensor_scalar(normed(t)[0:rows], h[0:rows, t, :], stats[0:rows, 9 + t:10 + t], None,
                                              ALU.mult), "pool_normed")
                dve.wait_ge(S("pads_ready"), 3)
                for n, psum, k, blocks, at, cols in transposed(TILES):
                    dve.wait_ge(S("pool_t"), n + 1)
                    gain = vec[:, G_MIX0 + k:G_MIX0 + k + blocks].unsqueeze(2).broadcast_to([P, blocks, cols])
                    step(dve, v.tensor_tensor(seq[0][:, k:k + blocks, META + at:META + at + cols], psum, gain,
                                              ALU.mult), "pool_t_out")
                sums = [seq[0], seq[1], seq[2], seq[1], seq[2]]
                for g in range(POOL_GROUPS):
                    src, to, w, k = sums[g], sums[g + 1], 2 ** g, 2 * g
                    step(dve, v.tensor_tensor(to[:, k:KD, META:PADL], src[:, k:KD, META:PADL],
                                              src[:, k:KD, META - w:PADL - w], ALU.add), "dve_order")
                    r = ratio[:, g, :].unsqueeze(1).broadcast_to([P, 2, META])
                    part = work[:, 0, 0:2 * META].rearrange("p (a n) -> p a n", a=2)
                    body = to[:, k:k + 2, :]
                    step(dve, v.tensor_tensor(part, body[:, :, META:2 * META], r, ALU.mult), "dve_order")
                    for lo, n, s in ((0, META, part), (META, T, body[:, :, 2 * META:])):
                        step(dve, v.scalar_tensor_tensor(pooled[:, k:k + 2, lo:lo + n], s, 0.5 ** (g + 1),
                                                         seq[0][:, k:k + 2, META + lo:META + lo + n],
                                                         ALU.mult, ALU.subtract), "pooled")
                dve.wait_ge(S("gain0_loaded"), 32)

                def add_mixed(n):
                    rows, t, _ = TILES[n]
                    dve.wait_ge(S("mixed"), n + 1)
                    to = tmp_m if t == NT else tmp[:, t, :]
                    step(dve, v.tensor_tensor(to, tile_banks(t), gb[0:rows, 0, :], ALU.mult), "dve_order")
                    step(dve, v.tensor_tensor(h[0:rows, t, :], h[0:rows, t, :], to, ALU.add), "h1")

                add_mixed(0)
                add_mixed(1)
                peer_norm_dve(dve, 0, "ffn0", gb[:, 1, :], "gain1_loaded", lambda: add_mixed(2))
                peer_vector(dve, 0, "ffn0")

            @block.tensor
            def _(pe):
                m = nc.tensor
                pe_transposes(pe, TILES, "pool")
                pe.wait_ge(S("pool_t_out"), 5)
                pe.wait_ge(S("pool_w_loaded"), 16)
                pe.wait_ge(S("pooled"), 2 * POOL_GROUPS)
                for n, (rows, t, at) in enumerate(TILES):
                    for g in range(POOL_GROUPS):
                        for k in range(2):
                            last = m.matmul(tile_banks(t)[:, GW * g:GW * (g + 1)], pooled[:, 2 * g + k, at:at + rows],
                                            poolw[:, 2 * g + k, :], start=(k == 0), stop=(k == 1))
                    last.then_inc(S("mixed"), 1)
                peer_scores_pe(pe, 0, "ffn0")
                peer_tensor(pe, 0, "ffn0")

        forget({"gain0_loaded", "dve_order", "waits_passed"})

        with nc.Block() as block:
            KV1_TILES = [(P, 1, KV0)]
            z_banks = cut(bank(0, 2), 0, 2, BANK)[:, :, 0:Z]
            wt_banks = cut(bank(2, 2), 0, 2, BANK)[:, :, 0:3 * P]
            wt_meta_banks = cut(bank(4, 2), 0, 2, BANK)[:, :, 0:T]

            def at_least(engine, name, value):
                if not (isinstance(value, int) and value <= 0):
                    engine.wait_ge(S(name), value)

            def over_pairs(engine, parts, ahead):
                def at(i, par):
                    for part, by in zip(parts, ahead):
                        if not isinstance(i, int) or 0 <= i + by < KD:
                            part(i + by, (par + by) % 2)

                for i in range(-2, 2):
                    at(i, i % 2)
                with engine.Fori(1, KD // 2 - 1) as ii:
                    for par in range(2):
                        at(ii * 2 + par, par)
                for i in range(KD - 2, KD + 1):
                    at(i, i % 2)

            @block.sync
            def _(sp):
                sp.dma_start(wq_att, w_q[0].rearrange("(k p) n -> p k n", p=P)).then_inc(S("w_q_loaded"), 16)
                sp.wait_ge(S("v_done"), 2)
                sp.dma_start(wq_peer, peer_wq[1].rearrange("(k p) n -> p k n", p=P)).then_inc(S("peer_wq1_loaded"), 16)
                sp.wait_ge(S("kq_out"), 2 * KD)
                sp.dma_start(wo_att, w_o[0].rearrange("(k p) n -> p k n", p=P)).then_inc(S("w_o_loaded"), 16)
                sp.dma_start(keys_in[1], peer_keys[1].rearrange("h w n c -> n (h w) c"))\
                    .then_inc(S("peer_keys1_loaded"), 16)
                out_v = out[0].rearrange("(t p) d -> p t d", p=P)
                for t in range(NT):
                    sp.wait_ge(S("tile_out1"), t + 1)
                    sp.dma_start(out_v[:, t, :], h[:, t, :]).then_inc(S("out_stored"), 16)
                sp.wait_ge(S("out_stored"), 16 * NT)

            @block.gpsimd
            def _(pool):
                g = nc.gpsimd
                step(pool, g.memset(neg_mask, 0.0), "masks_ready")
                for at in (META, Z - P):
                    step(pool, g.affine_select(out=neg_mask[:, at:at + P], in_=neg_mask[:, at:at + P],
                                               compare_op=ALU.is_gt, fill=NEG, base=0, pattern=[[-1, P]],
                                               channel_multiplier=1), "masks_ready")
                step(pool, g.memset(seg, 1.0), "masks_ready")
                step(pool, g.memset(seg[:, META + P - 1:META + P], 0.0), "masks_ready")
                pool.wait_ge(S("v_out"), 2)
                pool.wait_ge(S("kq_out"), 2 * KD)

                def stage_kq(i, par):
                    at_least(pool, "z_done", i - 1)
                    passed(pool)
                    g.tensor_copy(k_now[:, par:par + 1, :], k_t[:, bass.ds(i, 1), :])
                    g.tensor_copy(q_now[:, par:par + 1, :], q_t[:, bass.ds(i, 1), :]).then_inc(S("kq_staged"), 1)

                def stage_v(i, par):
                    at_least(pool, "pv_done", i - 1)
                    passed(pool)
                    g.tensor_copy(v_now[0:META, par, 2, :], v_meta[:, bass.ds(i * P, P)])
                    g.tensor_copy(v_now[:, par, 0:NT, :], hn[:, :, bass.ds(i * P, P)]).then_inc(S("v_staged"), 1)

                over_pairs(pool, (stage_kq, stage_v), (2, 0))
                peer_gpsimd(pool, 1, "ffn1")

            @block.scalar
            def _(act):
                a = nc.scalar
                act_squares(act, KV1_TILES, None, "kv1")

                kq_square(act, "kq", 0)
                for n in range(1, KD + 1):
                    kq_square(act, "kq", n)
                    kq_root(act, "kq", n - 1)
                for half in range(2):
                    act.wait_ge(S("v_done"), half + 1)
                    step(act, a.activation(hn[:, 1, BANK * half:BANK * (half + 1)], bank(2 + half), ACT.Copy), "v_out")
                for n in range(KD + 1, 2 * KD + 1):
                    if n < 2 * KD:
                        kq_square(act, "kq", n)
                    kq_root(act, "kq", n - 1)

                def softplus_part(i, par):
                    act.wait_ge(S("z_masked"), i + 1)
                    l = ls[:, 2 * par:2 * par + 2, :]
                    a.activation(l, zs[:, 2 * par:2 * par + 2, :], ACT.Abs)
                    act.drain()
                    a.activation(l, l, ACT.Exp, scale=-1.0)
                    act.drain()
                    a.activation(l, l, ACT.Ln, bias=1.0).then_inc(S("log_done"), 1)

                def weights(i, par):
                    act.wait_ge(S("log_w"), i + 1)
                    a.activation(ws[:, 2 * par:2 * par + 2, :], zs[:, 2 * par:2 * par + 2, :], ACT.Exp)\
                        .then_inc(S("w_ready"), 1)

                def meta_weights_out(i, par):
                    act.wait_ge(S("wt_done"), i + 1)
                    at_least(act, "pv_done", i)
                    a.activation(wt_meta[0:META], wt_meta_banks[0:META], ACT.Copy).then_inc(S("wt_meta_out"), 1)

                def y_out(i, par):
                    act.wait_ge(S("pv_done"), i + 1)
                    passed(act)
                    a.activation(att_y[:, bass.ds(i, 1), :], cut(bank(6 + par), 0, 1, T), ACT.Copy)\
                        .then_inc(S("att_y_out"), 1)

                over_pairs(act, (softplus_part, weights, meta_weights_out, y_out), (2, 1, 0, -1))
                act_squares(act, X_TILES, "h3", "ffn1")
                peer_queries_act(act, 1, "ffn1")
                peer_scalar(act, 1, "ffn1")

            @block.vector
            def _(dve):
                v = nc.vector
                dve_inverse_rms(dve, 0, P, 1, "kv1")
                step(dve, v.tensor_scalar(hn[:, 1, :], h[:, 1, :], stats[:, 10:11], None, ALU.mult), "kv1_normed")
                kv_inputs(dve, KV1_TILES, "kv1")
                step(dve, v.tensor_scalar(vec[:, V_Q:V_Q + 1], vec[:, V_Q:V_Q + 1], HD ** -0.5, None, ALU.mult),
                     "dve_order")
                for n in range(2 * KD):
                    kq_out(dve, "kq", n)
                dve.wait_ge(S("masks_ready"), 5)

                def mask(i, par):
                    dve.wait_ge(S("z_done"), i + 1)
                    at_least(dve, "w_ready", i - 1)
                    v.tensor_tensor(zs[:, 2 * par:2 * par + 2, :], z_banks, neg_mask.unsqueeze(1).broadcast_to([P, 2, Z]),
                                    ALU.add).then_inc(S("z_masked"), 1)

                def log_weights(i, par):
                    z, l, s = (x[:, 2 * par:2 * par + 2, :] for x in (zs, ls, ws))
                    dve.wait_ge(S("log_done"), i + 1)
                    v.scalar_tensor_tensor(l, z, 0.0, l, ALU.max, ALU.add)
                    dve.drain()
                    for e in range(2):
                        v.tensor_tensor_scan(s[:, e, ::-1], seg[:, ::-1], l[:, e, ::-1], 0.0, ALU.mult, ALU.add)
                    dve.drain()
                    v.tensor_tensor(z, z, s, ALU.subtract).then_inc(S("log_w"), 1)

                def weights_out(i, par):
                    dve.wait_ge(S("wt_done"), i + 1)
                    at_least(dve, "pv_done", i)
                    v.tensor_copy(wt, wt_banks).then_inc(S("wt_out"), 1)

                over_pairs(dve, (mask, log_weights, weights_out), (2, 1, 0))
                def add_attended(t):
                    dve.wait_ge(S("att_projected"), t + 1)
                    step(dve, v.tensor_tensor(h[:, t, :], h[:, t, :], bank(2 * t, 2), ALU.add), "h3")

                add_attended(0)
                peer_norm_dve(dve, 1, "ffn1", gb[:, 0, :], "gain0_loaded", lambda: add_attended(1))
                peer_vector(dve, 1, "ffn1")

            @block.tensor
            def _(pe):
                m = nc.tensor
                pe_transposes(pe, KV1_TILES, "kv1")
                pe.wait_ge(S("kv1_t_out"), 4)
                kq_project(pe, "kq", 0)
                for n in range(1, KD):
                    kq_project(pe, "kq", n)
                    kq_mean(pe, "kq", n - 1)
                for half in range(2):
                    v_product(pe, kv_in1, P, half, bank(2 + half), "v_done")
                    if half == 0:
                        kq_mean(pe, "kq", KD - 1)
                pe.wait_ge(S("w_q_loaded"), 16)
                kq_project(pe, "kq", KD)
                for n in range(KD + 1, 2 * KD):
                    kq_project(pe, "kq", n)
                    kq_mean(pe, "kq", n - 1)
                kq_mean(pe, "kq", 2 * KD - 1)

                pe.wait_ge(S("kq_roots"), 2 * KD)
                pe.wait_ge(S("kq_out"), 2 * KD)

                def z(i, par):
                    pe.wait_ge(S("kq_staged"), i + 1)
                    at_least(pe, "z_masked", i)
                    for e in range(2):
                        r = HD * e
                        for t, (lo, keys) in enumerate(((0, META + P), (META + P, L))):
                            last = m.matmul(bank(e)[:, lo:lo + keys], q_now[r:r + HD, par, P * t:P * (t + 1)],
                                            k_now[r:r + HD, par, 0:keys], start=True, stop=True)
                    last.then_inc(S("z_done"), 1)

                def transpose_weights(i, par):
                    pe.wait_ge(S("w_ready"), i + 1)
                    at_least(pe, "wt_out", i)
                    at_least(pe, "wt_meta_out", i)
                    for e in range(2):
                        w = ws[:, 2 * par + e, :]
                        m.transpose(bank(4 + e)[0:META, 0:P], w[:, 0:META], ident[:])
                        m.transpose(bank(4 + e)[0:META, P:T], w[:, META + P:2 * META + P], ident[:])
                        for to, at in ((0, META), (P, 2 * META + P), (2 * P, 2 * META + 2 * P)):
                            last = m.transpose(bank(2 + e)[:, to:to + P], w[:, at:at + P], ident[:])
                    last.then_inc(S("wt_done"), 1)

                def pv(i, par):
                    pe.wait_ge(S("v_staged"), i + 1)
                    pe.wait_ge(S("wt_out"), i + 1)
                    pe.wait_ge(S("wt_meta_out"), i + 1)
                    at_least(pe, "att_y_out", i - 1)
                    for e in range(2):
                        r = HD * e
                        y = bank(6 + par)[r:r + HD, 0:T]
                        v0, v1, vm = v_now[:, par, 0, r:r + HD], v_now[:, par, 1, r:r + HD], v_now[0:META, par, 2, r:r + HD]
                        m.matmul(y[:, 0:P], v0, wt[:, e, 0:P], start=True, stop=False)
                        m.matmul(y[:, 0:P], vm, wt_meta[0:META, e, 0:P], start=False, stop=True)
                        m.matmul(y[:, P:T], v0, wt[:, e, P:T], start=True, stop=False)
                        m.matmul(y[:, P:T], v1, wt[:, e, T:3 * P], start=False, stop=False)
                        last = m.matmul(y[:, P:T], vm, wt_meta[0:META, e, P:T], start=False, stop=True)
                    last.then_inc(S("pv_done"), 1)

                over_pairs(pe, (z, pv, transpose_weights), (2, -1, 0))
                pe.wait_ge(S("w_o_loaded"), 16)
                pe.wait_ge(S("att_y_out"), KD)
                for t in range(NT):
                    for half in range(2):
                        for k in range(KD):
                            last = m.matmul(bank(2 * t + half), att_y[:, k, P * t:P * (t + 1)],
                                            wo_att[:, k, BANK * half:BANK * (half + 1)],
                                            start=(k == 0), stop=(k == KD - 1))
                    last.then_inc(S("att_projected"), 1)
                peer_scores_pe(pe, 1, "ffn1")
                peer_tensor(pe, 1, "ffn1")


_INS = ["x", "pre_mix_g", "w_in", "conf_dw_w", "conf_dw_b", "conf_gn_g", "conf_gn_b", "sconv_w", "lru_conv_w",
        "lru_conv_b", "lru_wa", "lru_ba", "lru_wx", "lru_bx", "lru_lam", "w_out", "post_mix_g", "pre_mlp_g", "mlp_w1",
        "mlp_w2", "post_mlp_g", "meta_tokens_2", "norm_mix_2", "norm_ffn_2", "pool_w_2", "pool_scale_2", "kv_norm_2",
        "w_kv_2", "k_norm_2", "w_q_2", "q_norm_2", "w_o_2", "peer_wq_2", "peer_keys_2", "peer_u_2", "peer_v_2"]


def kernel(**inputs):
    import numpy as np
    import concourse.bacc as bacc
    from concourse.bass_utils import run_bass_kernel_spmd

    nc = bacc.Bacc("TRN2", target_bir_lowering=False, num_devices=1)
    arrays, args = {}, []
    for name in _INS:
        a = np.ascontiguousarray(inputs[name])
        arrays[f"in_{name}"] = a
        args.append(nc.dram_tensor(f"in_{name}", a.shape, mybir.dt.from_np(a.dtype), kind="ExternalInput").ap())
    args.append(nc.dram_tensor("out", (1, T, D), F32, kind="ExternalOutput").ap())
    program(nc, *args)
    return run_bass_kernel_spmd(nc, [arrays], core_ids=[0]).results[0]["out"]
```
